# Optimizing a Trainium2 kernel written in Bass

```python
import math
import jax, jax.numpy as jnp
from jax import lax
import numpy as np

D_MODEL = 1024
BATCH = 1
SEQ = 512
DEPTH = 1

SSM_WIDTH = 512
SSM_GROUP = 16
SSM_GROUPS = SSM_WIDTH // SSM_GROUP
SSM_STATE = 64
DT_MIN = 1e-3
DT_MAX = 1e-1
N_HEADS = 8
HEAD_DIM = 64
ATTN_WIDTH = N_HEADS * HEAD_DIM
IDX_HEADS = 8
IDX_DIM = 64
TOPK_MAX = 256
Q_BLOCK = 128
N_EXPERTS = 64
TOP_K = 8
N_GROUPS = 8
TOPK_GROUPS = 4
EXPERT_DIM = 256
SHARED_DIM = 256
ROUTED_SCALE = 2.5
DISPATCH_BLOCK = 128
EPS = 1e-6

IN_SPLIT_SIZES = (SSM_WIDTH, ATTN_WIDTH, HEAD_DIM, HEAD_DIM, IDX_HEADS * IDX_DIM, IDX_DIM, IDX_HEADS, D_MODEL, D_MODEL)
IN_WIDTH = SSM_WIDTH + ATTN_WIDTH + 2 * HEAD_DIM + IDX_HEADS * IDX_DIM + IDX_DIM + IDX_HEADS + 2 * D_MODEL

kernel_name = "hybrid_s5_dsa_moe_adaln_block"

def rms_norm(x, g):
    xf = x.astype(jnp.float32)
    y = xf * lax.rsqrt(jnp.mean(xf * xf, axis=-1, keepdims=True) + EPS)
    return (y * g.astype(jnp.float32)).astype(x.dtype)

def modulate(x, g, shift, scale):
    return rms_norm(x, g) * (1.0 + scale) + shift

def alibi_slopes(n):
    return 2.0 ** (-8.0 * (jnp.arange(n, dtype=jnp.float32) + 1.0) / n)

def _complex_linear_combine(e1, e2):
    a1r, a1i, b1r, b1i = e1
    a2r, a2i, b2r, b2i = e2
    return (a1r * a2r - a1i * a2i,
            a1r * a2i + a1i * a2r,
            a2r * b1r - a2i * b1i + b2r,
            a2r * b1i + a2i * b1r + b2i)

def s5_mixer(u, lam_re, lam_im, log_dt, b_re, b_im, c_re, c_im, d_skip, w_glu, b_glu):
    bsz, seq, _ = u.shape
    f32 = jnp.float32
    uf = u.astype(f32)
    ug = uf.reshape(bsz, seq, SSM_GROUPS, SSM_GROUP)
    dt = jnp.exp(log_dt.astype(f32))[:, None]
    lr = lam_re.astype(f32)
    li = lam_im.astype(f32)
    mag = jnp.exp(lr * dt)
    a_re = mag * jnp.cos(li * dt)
    a_im = mag * jnp.sin(li * dt)
    den = lr * lr + li * li
    n_re = a_re - 1.0
    f_re = (n_re * lr + a_im * li) / den
    f_im = (a_im * lr - n_re * li) / den
    br = b_re.astype(f32)
    bi = b_im.astype(f32)
    bb_re = f_re[..., None] * br - f_im[..., None] * bi
    bb_im = f_re[..., None] * bi + f_im[..., None] * br
    bu_re = jnp.einsum('blgh,gph->lbgp', ug, bb_re)
    bu_im = jnp.einsum('blgh,gph->lbgp', ug, bb_im)
    shape_a = (seq, 1, SSM_GROUPS, SSM_STATE)
    a_re_t = jnp.broadcast_to(a_re, shape_a)
    a_im_t = jnp.broadcast_to(a_im, shape_a)
    _, _, h_re, h_im = lax.associative_scan(_complex_linear_combine, (a_re_t, a_im_t, bu_re, bu_im), axis=0)
    y = (jnp.einsum('ghp,lbgp->blgh', c_re.astype(f32), h_re)
         - jnp.einsum('ghp,lbgp->blgh', c_im.astype(f32), h_im))
    y = y.reshape(bsz, seq, SSM_WIDTH) + d_skip.astype(f32) * uf
    y = jax.nn.gelu(y)
    y = y * jax.nn.sigmoid(y @ w_glu.astype(f32) + b_glu.astype(f32))
    return y.astype(u.dtype)

def dsa_attention(q, k, v, q_idx, k_idx, w_idx):
    bsz, seq = q.shape[0], q.shape[1]
    f32 = jnp.float32
    topk = min(TOPK_MAX, seq // 4)
    n_blocks = seq // Q_BLOCK
    slopes = alibi_slopes(N_HEADS)
    key_pos = jnp.arange(seq)
    kf = k_idx.astype(f32)

    def to_blocks(a):
        return a.reshape((bsz, n_blocks, Q_BLOCK) + a.shape[2:]).swapaxes(0, 1)

    def block(args):
        qb, qib, wb, blk = args
        q_pos = blk * Q_BLOCK + jnp.arange(Q_BLOCK)
        s_idx = jnp.einsum('bqhd,bsd->bqhs', qib.astype(f32), kf) * (IDX_DIM ** -0.5)
        score = jnp.einsum('bqh,bqhs->bqs', wb.astype(f32) * (IDX_HEADS ** -0.5), jax.nn.relu(s_idx))
        causal = key_pos[None, :] <= q_pos[:, None]
        score = jnp.where(causal[None], score, -jnp.inf)
        _, sel = lax.top_k(score, topk)
        k_sel = jax.vmap(lambda kk, ii: kk[ii])(k, sel)
        v_sel = jax.vmap(lambda vv, ii: vv[ii])(v, sel)
        logits = jnp.einsum('bqhd,bqkd->bhqk', qb, k_sel).astype(f32) * (HEAD_DIM ** -0.5)
        dist = (q_pos[None, :, None] - sel).astype(f32)
        logits = logits - slopes[None, :, None, None] * dist[:, None]
        valid = sel <= q_pos[None, :, None]
        logits = jnp.where(valid[:, None], logits, -jnp.inf)
        p = jax.nn.softmax(logits, axis=-1).astype(v.dtype)
        return jnp.einsum('bhqk,bqkd->bqhd', p, v_sel)

    out = lax.map(block, (to_blocks(q), to_blocks(q_idx), to_blocks(w_idx), jnp.arange(n_blocks)))
    return out.swapaxes(0, 1).reshape(bsz, seq, ATTN_WIDTH)

def moe_ffn(u, w_router, router_bias, w_gate, w_up, w_down, ws_gate, ws_up, ws_down):
    bsz, seq, d = u.shape
    f32 = jnp.float32
    xt = u.reshape(-1, d)
    n_tok = xt.shape[0]
    scores = jax.nn.sigmoid(xt.astype(f32) @ w_router.astype(f32))
    biased = scores + router_bias.astype(f32)
    per_group = N_EXPERTS // N_GROUPS
    group_score = lax.top_k(biased.reshape(n_tok, N_GROUPS, per_group), 2)[0].sum(-1)
    _, gsel = lax.top_k(group_score, TOPK_GROUPS)
    gmask = jnp.any(gsel[:, :, None] == jnp.arange(N_GROUPS)[None, None, :], axis=1)
    emask = jnp.repeat(gmask, per_group, axis=1)
    _, eidx = lax.top_k(jnp.where(emask, biased, -jnp.inf), TOP_K)
    gate = jnp.take_along_axis(scores, eidx, axis=1)
    gate = gate / jnp.sum(gate, axis=-1, keepdims=True) * ROUTED_SCALE

    n_assign = n_tok * TOP_K
    e_flat = eidx.reshape(-1)
    t_flat = jnp.repeat(jnp.arange(n_tok, dtype=jnp.int32), TOP_K)
    g_flat = gate.reshape(-1)
    order = jnp.argsort(e_flat)
    e_s = e_flat[order]
    t_s = t_flat[order]
    g_s = g_flat[order]
    counts = jnp.bincount(e_flat, length=N_EXPERTS)
    padded = (counts + DISPATCH_BLOCK - 1) // DISPATCH_BLOCK * DISPATCH_BLOCK
    start = jnp.cumsum(counts) - counts
    pend = jnp.cumsum(padded)
    pstart = pend - padded
    dest = pstart[e_s] + jnp.arange(n_assign) - start[e_s]
    n_blocks = (n_assign + N_EXPERTS * (DISPATCH_BLOCK - 1) + DISPATCH_BLOCK - 1) // DISPATCH_BLOCK
    total = n_blocks * DISPATCH_BLOCK
    tok_pad = jnp.zeros((total,), jnp.int32).at[dest].set(t_s)
    gate_pad = jnp.zeros((total,), f32).at[dest].set(g_s)
    blk_expert = jnp.minimum(jnp.searchsorted(pend, jnp.arange(n_blocks) * DISPATCH_BLOCK, side='right'), N_EXPERTS - 1)

    def step(acc, blk):
        tok, g, e = blk
        xb = xt[tok]
        hb = jax.nn.silu(xb @ w_gate[e]) * (xb @ w_up[e])
        yb = (hb @ w_down[e]).astype(f32) * g[:, None]
        return acc.at[tok].add(yb), None

    routed, _ = lax.scan(step, jnp.zeros((n_tok, d), f32),
                         (tok_pad.reshape(n_blocks, DISPATCH_BLOCK), gate_pad.reshape(n_blocks, DISPATCH_BLOCK), blk_expert))
    shared = (jax.nn.silu(xt @ ws_gate) * (xt @ ws_up)) @ ws_down
    return (routed + shared.astype(f32)).astype(u.dtype).reshape(bsz, seq, d)

def setup_inputs(seed: int = 0) -> dict:
    key = jax.random.key(seed)
    ks = iter(jax.random.split(key, 40))
    f32 = jnp.float32

    def nrm(shape, s):
        return jax.random.normal(next(ks), shape, f32) * s

    L = DEPTH
    d = D_MODEL
    lam_im_base = math.pi * jnp.arange(SSM_STATE, dtype=f32)
    return {
        "x": nrm((BATCH, SEQ, d), 1.0),
        "c": nrm((BATCH, d), 1.0),
        "w_ada": nrm((L, d, 6 * d), 0.5 * d ** -0.5),
        "b_ada": nrm((L, 6 * d), 0.02),
        "norm1_g": 1.0 + nrm((L, d), 0.02),
        "w_in": nrm((L, d, IN_WIDTH), d ** -0.5),
        "ssm_lambda_re": -0.5 + nrm((L, SSM_GROUPS, SSM_STATE), 0.01),
        "ssm_lambda_im": lam_im_base + nrm((L, SSM_GROUPS, SSM_STATE), 0.01),
        "ssm_log_dt": jax.random.uniform(next(ks), (L, SSM_GROUPS), f32, math.log(DT_MIN), math.log(DT_MAX)),
        "ssm_b_re": nrm((L, SSM_GROUPS, SSM_STATE, SSM_GROUP), (2.0 * SSM_GROUP) ** -0.5),
        "ssm_b_im": nrm((L, SSM_GROUPS, SSM_STATE, SSM_GROUP), (2.0 * SSM_GROUP) ** -0.5),
        "ssm_c_re": nrm((L, SSM_GROUPS, SSM_GROUP, SSM_STATE), (2.0 * SSM_STATE) ** -0.5),
        "ssm_c_im": nrm((L, SSM_GROUPS, SSM_GROUP, SSM_STATE), (2.0 * SSM_STATE) ** -0.5),
        "ssm_d": nrm((L, SSM_WIDTH), 1.0),
        "ssm_w_glu": nrm((L, SSM_WIDTH, SSM_WIDTH), SSM_WIDTH ** -0.5),
        "ssm_b_glu": nrm((L, SSM_WIDTH), 0.02),
        "w_proj_ssm": nrm((L, SSM_WIDTH, d), SSM_WIDTH ** -0.5),
        "w_proj_attn": nrm((L, ATTN_WIDTH, d), ATTN_WIDTH ** -0.5),
        "w_out": nrm((L, d, d), d ** -0.5),
        "norm2_g": 1.0 + nrm((L, d), 0.02),
        "w_router": nrm((L, d, N_EXPERTS), d ** -0.5),
        "router_bias": nrm((L, N_EXPERTS), 0.01),
        "w_exp_gate": nrm((L, N_EXPERTS, d, EXPERT_DIM), d ** -0.5),
        "w_exp_up": nrm((L, N_EXPERTS, d, EXPERT_DIM), d ** -0.5),
        "w_exp_down": nrm((L, N_EXPERTS, EXPERT_DIM, d), EXPERT_DIM ** -0.5),
        "w_sh_gate": nrm((L, d, SHARED_DIM), d ** -0.5),
        "w_sh_up": nrm((L, d, SHARED_DIM), d ** -0.5),
        "w_sh_down": nrm((L, SHARED_DIM, d), SHARED_DIM ** -0.5),
        "norm_f_g": 1.0 + nrm((d,), 0.02),
    }

def reference(x, c, w_ada, b_ada, norm1_g, w_in, ssm_lambda_re, ssm_lambda_im, ssm_log_dt,
              ssm_b_re, ssm_b_im, ssm_c_re, ssm_c_im, ssm_d, ssm_w_glu, ssm_b_glu,
              w_proj_ssm, w_proj_attn, w_out, norm2_g, w_router, router_bias,
              w_exp_gate, w_exp_up, w_exp_down, w_sh_gate, w_sh_up, w_sh_down, norm_f_g):
    bsz, seq, _ = x.shape
    offsets = [int(o) for o in np.cumsum(IN_SPLIT_SIZES)[:-1]]
    h = x
    for layer in range(DEPTH):
        ada = jax.nn.silu(c) @ w_ada[layer] + b_ada[layer]
        shift1, scale1, gate1, shift2, scale2, gate2 = jnp.split(ada[:, None, :], 6, axis=-1)

        u = modulate(h, norm1_g[layer], shift1, scale1)
        proj = u @ w_in[layer]
        u_ssm, q, k, v, q_idx, k_idx, w_idx, g_ssm, g_attn = jnp.split(proj, offsets, axis=-1)
        y_ssm = s5_mixer(u_ssm, ssm_lambda_re[layer], ssm_lambda_im[layer], ssm_log_dt[layer],
                         ssm_b_re[layer], ssm_b_im[layer], ssm_c_re[layer], ssm_c_im[layer],
                         ssm_d[layer], ssm_w_glu[layer], ssm_b_glu[layer])
        y_attn = dsa_attention(q.reshape(bsz, seq, N_HEADS, HEAD_DIM), k, v,
                               q_idx.reshape(bsz, seq, IDX_HEADS, IDX_DIM), k_idx, w_idx)
        mixed = (jax.nn.sigmoid(g_ssm) * (y_ssm @ w_proj_ssm[layer])
                 + jax.nn.sigmoid(g_attn) * (y_attn @ w_proj_attn[layer]))
        h = h + gate1 * (mixed @ w_out[layer])

        u2 = modulate(h, norm2_g[layer], shift2, scale2)
        h = h + gate2 * moe_ffn(u2, w_router[layer], router_bias[layer], w_exp_gate[layer], w_exp_up[layer],
                                w_exp_down[layer], w_sh_gate[layer], w_sh_up[layer], w_sh_down[layer])
    return rms_norm(h, norm_f_g)


_drawn_inputs = setup_inputs


def setup_inputs(seed=0):
    import zlib

    import numpy as np

    out = dict(_drawn_inputs(seed))
    spreads = {}
    factors = {'norm1_g': 2.786,
     'ssm_lambda_re': 64.0,
     'ssm_lambda_im': 36.872,
     'ssm_log_dt': 36.656,
     'ssm_b_re': 39.096,
     'ssm_b_im': 32.24,
     'ssm_c_re': 46.52,
     'ssm_c_im': 43.848,
     'ssm_b_glu': 23.401,
     'norm_f_g': 7.509}
    for name, (base, spread) in spreads.items():
        noise = np.random.default_rng([zlib.crc32(name.encode()), seed]).standard_normal(out[name].shape)
        drawn = base * np.exp(spread * noise) if base else spread * noise
        out[name] = __import__('jax').numpy.asarray(drawn.astype(out[name].dtype))
    for name, factor in factors.items():
        out[name] = (out[name] * factor).astype(out[name].dtype)
    return out
```

```python
import math
from contextlib import ExitStack

import concourse.bass as bass
from concourse import mybir

F32 = mybir.dt.float32
I32 = mybir.dt.int32
ALU = mybir.AluOpType
ACT = mybir.ActivationFunctionType
AX = mybir.AxisListType

P = 128
SEQ, DM = 512, 1024
TT, KD = SEQ // P, DM // P
G, GH, NS = 32, 16, 64
SW = G * GH
CH = 8
NC = SEQ // CH
NQ, QG = 4, G // 4
NH, HD = 8, 64
TOPK = min(256, SEQ // 4)
NE, EK, NGR, TG, ED = 64, 8, 8, 4, 256
EPG = NE // NGR
EPS = 1e-6
ROUTED_SCALE = 2.5
MASKED, TAKEN, LIM = -1.0e30, -3.0e38, -2.0e38
MAGIC = 12582912.0
TWO_PI = 2 * math.pi
C1 = 6.28125
C2 = 1.9350051879882812e-03
C3 = TWO_PI - C1 - C2
SIN_MAX = 3.1415925
NB = 6
RING = 4
NEP = NE + RING
MAXOV = SEQ * EK // (P + 1)
XB = SEQ // P - 1
O_SSM, O_Q, O_K, O_V, O_QI, O_KI, O_WI, O_GS, O_GA = 0, 512, 1024, 1088, 1152, 1664, 1728, 1736, 2760


def groups_in_order():
    def s5_build(q):
        return [("bT", q, n) for n in range(2)] + [("K", q, n) for n in range(2)]

    def s5_apply(q):
        return [("uc", q), ("v1", q), ("v2", q)] + [("y", q, n) for n in range(2)]

    o = [("lam", 0)] + [("cT", j) for j in range(4)]
    o += [("ada", n) for n in range(4)]
    o += [("uT", t, n) for t in range(TT) for n in range(2)]
    o += [("ssm", t) for t in range(TT)]
    o += s5_build(0) + [("kiT", 0), ("kT", 0), ("vw", 0)] + s5_apply(0)
    o += [("qiT", m) for m in range(4)] + [("idx", 1, h) for h in range(NH)]
    o += s5_build(1) + [("idx", 2, h) for h in range(NH)] + s5_apply(1)
    o += [("idx", 3, h) for h in range(NH)]
    o += s5_build(2) + [("qT", m) for m in range(4)] + s5_apply(2) + s5_build(3)
    o += [("ada", n) for n in range(4, 12)]
    o += [("gs", d) for d in range(4)] + s5_apply(3)
    o += [("yT", m) for m in range(4)] + [("ga", d) for d in range(4)]
    for i in range(TT):
        o += [("lg", i, 0), ("lg", i, 1)]
        for h in range(NH):
            if h + 2 < NH:
                o.append(("lg", i, h + 2))
            o.append(("pT", i, h))
        o.append(("yaT", i))
    o += [("glu", m) for m in range(4)]
    o += [(n, d) for d in range(4) for n in ("ps", "pa")]
    o += [("gs", d) for d in range(4, 8)] + [("ga", d) for d in range(4, 8)]
    o += [(n, d) for d in range(4, 8) for n in ("ps", "pa")]
    o += [("out", t, n) for n in range(2) for t in range(TT)]
    o += [("u2T", t, n) for t in range(TT) for n in range(2)]
    o += [("rt", 0)] + [("sh", m) for m in range(4)] + [("pos", 0), ("cnt", 0)]
    o += [("dn", t, n) for t in range(TT) for n in range(2)]
    return o


BY_VECTOR = {"cT", "K", "ada", "v1", "v2", "lg", "ps", "pa", "out", "pos", "cnt", "dn"}
ORDER = {g: n for n, g in enumerate(groups_in_order())}
TAKEN_OUT = {}
for _g in ORDER:
    _v = _g[0] in BY_VECTOR or _g in (("sh", 2), ("sh", 3))
    TAKEN_OUT[_g] = (_v, 1 + sum(1 for v, _ in TAKEN_OUT.values() if v == _v))
AT = {n: g for g, n in ORDER.items()}


def stream_items():
    o = [("A", n) for n in range(4)] + [("ssm", 0)] + [("A", n) for n in range(4, 6)] + [("misc", 0)]
    o += [("A", n) for n in range(6, 9)] + [("qi", 0)] + [("A", n) for n in range(9, 12)] + [("q", 0)]
    o += [("gs", 0), ("ga", 0), ("glu", 0), ("pp", 0), ("gs", 1), ("ga", 1), ("pp", 1)]
    o += [("out", 0), ("out", 1), ("sh", 0), ("shd", 0)]
    return o


ITEMS = {g: n for n, g in enumerate(stream_items())}
LAST_USE = {("ssm", 0): ("ssm", 3), ("misc", 0): ("vw", 0), ("qi", 0): ("qiT", 3), ("q", 0): ("qT", 3),
            ("glu", 0): ("glu", 3), ("out", 0): ("out", 3, 0), ("out", 1): ("out", 3, 1), ("sh", 0): ("sh", 3)}
LAST_USE.update({(_n, _h): (_n if _n != "pp" else "pa", 4 * _h + 3) for _n in ("gs", "ga", "pp") for _h in range(2)})
DMAS = {"misc": 6, "pp": 2, "sh": 2, "shd": 2}


def a3(ap, n):
    return ap.rearrange("p (a b) -> p a b", a=n)


def build(nc, a, out):
    U2D = nc.dram_tensor("u2_rows", (SEQ, DM), F32, kind="Internal").ap()
    ACC = [nc.dram_tensor(f"expert_sum{n}", (SEQ + P, DM), F32, kind="Internal").ap() for n in range(2)]
    OVD = nc.dram_tensor("more_blocks", (MAXOV + 1, 3), I32, kind="Internal").ap()
    UD = nc.dram_tensor("u_ssm_rows", (SEQ, SW), F32, kind="Internal").ap()
    ctx = ExitStack()
    with ctx:
        def sb(name, shape, dt=F32):
            return ctx.enter_context(nc.sbuf_tensor(name, shape, dt))

        ring = sb("ring", [P, RING * 6144])
        strm = [ring[:, 4096 * s:4096 * (s + 1)] for s in range(3)]
        work = ring[:, 3 * 4096:RING * 6144]
        H = sb("H", [P, TT, DM])
        ADA = sb("ADA", [P, 6 * DM])
        uTs = sb("uTs", [P, KD * SEQ])
        uT = a3(uTs[:, :], KD)
        XT = sb("XT", [P, TT * DM])
        qT, qiT = a3(XT[:, 0:2048], 4), a3(XT[:, 2048:4096], 4)
        unat = a3(XT[:, 2048:4096], 4)
        yT, y2T = qiT, qT
        UB = sb("UB", [P, 4096])
        ut4 = a3(UB[:, :], TT)
        mixT = a3(UB[:, :], KD)
        kT = sb("kT", [P, SEQ])
        kiT = sb("kiT", [P, SEQ])
        vw = sb("vw", [P, TT, 72])
        GB = sb("GB", [P, DM])
        ident = sb("ident", [P, P])
        ones = sb("ones", [P, P])
        lower = sb("lower", [P, P])
        iota = sb("iota", [P, SEQ])
        sm = sb("sm", [P, 432])
        csil, c_in = sm[:, 0:8], sm[:, 8:16]
        ssq, rstd = sm[:, 16:20], sm[:, 20:24]
        sg, nsg = sm[:, 24:25], sm[:, 25:26]
        bglu = sm[:, 28:32]
        var, newt = sm[:, 244:248], sm[:, 248:252]
        wis = sm[:, 32:64].rearrange("p (t h) -> p t h", t=TT)
        mx, nb, rsum, rinv = sm[:, 64:96], sm[:, 96:128], sm[:, 128:160], sm[:, 160:192]
        tokid = sm[:, 192:196]
        dummy = sm[:, 196:197]
        pp1 = sm[:, 197:198]
        top8 = sm[:, 200:208]
        dsk = sm[0:GH, 208:240]
        junk1, junkp = sm[:, 240:241], sm[:, 242:243]
        kd = sm[0:GH, 300:428]
        score = sb("score", [P, 1152])
        sc_of = {1: score[:, 0:256], 2: score[:, 256:640], 3: score[:, 640:1152]}
        relu = a3(ADA[:, 0:1024], 2)
        K16s = sb("K16s", [P, 1024])
        K16 = K16s[0:GH, :]
        uperm = K16s[0:NC, :]
        lamn = K16s[0:G, 0:256]
        at = [0]

        def take(n):
            at[0] += n
            assert at[0] <= 12288
            return work[:, at[0] - n:at[0]]

        BA, W1, CA, W2, W3 = take(1024), take(1024), take(1152), take(1024), take(1024)
        uc, Vt = BA[:, 0:512], BA[:, 512:1024]
        COS, SIN = take(512), take(512)
        Xb, Zb, X, Z = take(512), take(512), take(512), take(512)
        T512, D0, GV, GC, GS = take(512), take(512), take(512), take(512), take(512)
        Are, AimS = take(9 * G), take(9 * G)
        lam, dtb, th, m8 = take(64), take(32), take(32), take(32)
        E9, A9, N9 = score[:, 0:288], score[:, 288:576], score[:, 576:864]
        fcol = [score[:, 864 + 32 * n:896 + 32 * n] for n in range(5)]
        cn = a3(XT[:, 0:1024], 8)
        B1, B2 = XT[:, 1024:1536], XT[:, 1536:2048]
        Mb = [work[:, 0:128], work[:, 128:384], work[:, 384:768], work[:, 768:1280]]
        tb = [work[:, 1280 + 512 * n:1792 + 512 * n] for n in range(3)]
        pTb = [work[:, 2816 + 512 * n:3328 + 512 * n] for n in range(2)]
        yat = work[:, 3840:4352]
        yaT = a3(work[:, 4352:6400], 4)
        sab = a3(work[:, 6400:8448], 4)
        tmpv = work[:, 8448:8960]
        tmp2 = ADA[:, 0:512]
        sgb = a3(ADA[:, 0:2048], 4)
        ps = [ctx.enter_context(nc.psum_tensor(f"ps{b}", [P, 512], F32)) for b in range(8)]

        S = {}
        for n in """x_in c_in b_in norm_in lam_in ct_in bt_in dt_in dsk_in bglu_in bias_in consts ada_zero
                c_silu dt_exp angles sines squares u_tile ada_sum pool_turn u_perm inverse root empties ov_em xz_ok b_ok ba_ok ca_ok w2_ok tables k_full toeplitz
                u_rows u_chunks rotated relu_free causal dist t_max prob av_done y_att y2_ok mixed h_out
                u2_tile u2_rows masks slots shared hbase heads
                group_done out_scalar out_vector vector_o scalar_o pool_o
                x_zero slot_hot list_done list_out x_tr x_out_s x_out_v gu_done g_silu h_ok hT_done hT_out expert_done
                y_out_s y_out_v ov_list ov_out ov_row ov_go ov_hot ov_ldone ov_idx ov_x ov_xt ov_xs ov_xv ov_gu
                ov_silu ov_h ov_ht ov_hts ov_y ov_yo ov_add all_added sums_joined fin_add fin_sq final out_done""".split():
            S[n] = ctx.enter_context(nc.semaphore(n))
        y_added = [ctx.enter_context(nc.semaphore(f"y_added{n}")) for n in range(2)]
        ov_w = [ctx.enter_context(nc.semaphore(f"ov_weights{n}")) for n in range(2)]
        gathered = [ctx.enter_context(nc.semaphore(f"gathered{n}")) for n in range(2)]
        sum_in = [ctx.enter_context(nc.semaphore(f"sum_in{t}")) for t in range(TT)]
        s_in = [ctx.enter_context(nc.semaphore(f"stream_in{s}")) for s in range(3)]
        w_in_sem = [ctx.enter_context(nc.semaphore(f"expert_in{s}")) for s in range(RING)]

        def bank(g):
            return ps[ORDER[g] % NB]

        def done(eng, g):
            eng.wait_ge(S["group_done"], ORDER[g] + 1)
            return bank(g)

        def taken(eng, g):
            v, n = TAKEN_OUT[g]
            eng.wait_ge(S["out_vector" if v else "out_scalar"], n)

        def takes(ins, g):
            return ins.then_inc(S["out_vector" if TAKEN_OUT[g][0] else "out_scalar"], 1)

        in_value, n_before = {}, [0, 0, 0]
        for g, n in ITEMS.items():
            n_before[n % 3] += 16 * DMAS.get(g[0], 1)
            in_value[g] = n_before[n % 3]

        def arrived(eng, g):
            n = ITEMS[g]
            eng.wait_ge(s_in[n % 3], in_value[g])
            return strm[n % 3]

        def unused(eng, g):
            if g[0] == "A":
                eng.wait_ge(S["ada_sum"], g[1] + 1)
            else:
                done(eng, LAST_USE[g])

        def bc(ap, n, axis):
            shape = list(ap.shape)
            return ap.unsqueeze(axis).broadcast_to(shape[:axis] + [n] + shape[axis:])

        win_k = a["w_in"][0].rearrange("(k p) n -> p k n", p=P)
        wada_k = a["w_ada"][0].rearrange("(p k) n -> p k n", k=KD)

        def rows(w):
            return w.rearrange("(k p) n -> p k n", p=P)

        slot_of = [2, 3, 0, 1]
        wgu = [ring[:, 6144 * s:6144 * s + 4096].rearrange("p (k n) -> p k n", k=KD) for s in slot_of]
        wdn = [ring[:, 6144 * s + 4096:6144 * (s + 1)].rearrange("p (k n) -> p k n", k=2) for s in slot_of]
        xg = [XT[:, 1024 * n:1024 * (n + 1)] for n in range(2)]
        xgT = [a3(XT[:, 2048 + 1024 * n:3072 + 1024 * n], KD) for n in range(2)]
        ye = [uTs[:, 1024 * n:1024 * (n + 1)] for n in range(2)]
        hot = [a3(uTs[:, 2048 + 512 * n:2560 + 512 * n], TT) for n in range(2)]
        hs, hg = uTs[:, 3072:3328], uTs[:, 3328:3584]
        hTe = a3(uTs[:, 3584:3840], 2)
        idx = sb("idx", [P, RING], I32)
        adx = sb("adx", [P, 2], I32)
        gat = sb("gat", [P, RING])
        empty = [sm[:, 280 + n:281 + n] for n in range(2)]
        RG = UB[:, 0:TT * NEP * 3].rearrange("p (t e c) -> p t e c", t=TT, c=3)
        posm = UB[:, 816:816 + TT * NEP].rearrange("p (t e) -> p t e", t=TT)
        scr = UB[:, 1088:4096]
        sct, bia, wk, Mm = (a3(scr[:, 256 * n:256 * (n + 1)], TT) for n in range(4))
        m2 = scr[:, 1024:1280].rearrange("p (t g k) -> p t g k", t=TT, g=NGR)
        gsum, rank, gm = (a3(scr[:, 1280 + 32 * n:1312 + 32 * n], TT) for n in range(3))
        cmp = scr[:, 1376:1632].rearrange("p (t g k) -> p t g k", t=TT, g=NGR)
        cmp2 = scr[:, 1632:1888].rearrange("p (t g k) -> p t g k", t=TT, g=NGR)
        rbias = scr[:, 1888:1952]
        lt8 = scr[:, 1952:2016].rearrange("p (a b) -> p a b", a=8)
        ovf, ovr, ovc, ovt = (scr[:, 2016 + 192 * n:2208 + 192 * n] for n in range(4))
        ovo = scr[:, 1376:1568]
        cnt, ovl = scr[:, 2784:2848], scr[:, 2848:2852]
        gsm = scr[:, 2852:2856]
        ovrow = sb("ovrow", [1, 3 * (MAXOV + 1) + 1], I32)
        ovi = sb("ovi", [P, 3], I32)
        assert MAXOV + 1 <= 32
        ADD0 = 16 * (TT + 1)

        def added(eng, blk, r):
            eng.wait_ge(y_added[r % 2], blk * (8 * RING) + (16 * (r // 2 + 1) + ADD0))

        def over_blocks(step, eng):
            for r in range(RING):
                step(0, r)
            with eng.Fori(1, NE // RING - 1) as blk:
                for r in range(RING):
                    step(blk, r)
            for r in range(RING):
                step(NE // RING - 1, r)

        def is_first(blk, r):
            return isinstance(blk, int) and RING * blk + r == 0

        def follows(blk, r, n):
            return not isinstance(blk, int) or RING * blk + r + n < NE

        block = ctx.enter_context(nc.Block())

        @block.sync
        def _(sp):
            def load(g):
                n = ITEMS[g]
                if n >= 3:
                    unused(sp, stream_items()[n - 3])
                slot, s, k = strm[n % 3], s_in[n % 3], g[0]
                if k == "A":
                    part, j = g[1] // 4, g[1] % 4
                    sp.dma_start(a3(slot, 2), wada_k[:, 2 * j:2 * j + 2, 2048 * part:2048 * (part + 1)]).then_inc(s, 16)
                elif k in ("ssm", "qi", "q", "gs", "ga"):
                    c0 = {"ssm": O_SSM, "qi": O_QI, "q": O_Q, "gs": O_GS, "ga": O_GA}[k] + 512 * g[1]
                    sp.dma_start(a3(slot, 8), win_k[:, :, c0:c0 + 512]).then_inc(s, 16)
                elif k == "misc":
                    v = a3(slot[:, 0:8 * 328], 8)
                    for c, c0, w in ((0, O_KI, 64), (64, O_KI, 64), (128, O_K, 64), (192, O_K, 64), (256, O_V, 64), (320, O_WI, 8)):
                        sp.dma_start(v[:, :, c:c + w], win_k[:, :, c0:c0 + w]).then_inc(s, 16)
                elif k == "glu":
                    sp.dma_start(a3(slot[:, 0:2048], 4), rows(a["ssm_w_glu"][0])).then_inc(s, 16)
                elif k == "pp":
                    for j, w in enumerate(("w_proj_ssm", "w_proj_attn")):
                        sp.dma_start(a3(slot[:, 2048 * j:2048 * (j + 1)], 4),
                                     rows(a[w][0])[:, :, 512 * g[1]:512 * (g[1] + 1)]).then_inc(s, 16)
                elif k == "out":
                    sp.dma_start(a3(slot, 8), rows(a["w_out"][0])[:, :, 512 * g[1]:512 * (g[1] + 1)]).then_inc(s, 16)
                elif k == "sh":
                    for j, w in enumerate(("w_sh_gate", "w_sh_up")):
                        sp.dma_start(a3(slot, 8)[:, :, 256 * j:256 * (j + 1)], rows(a[w][0])).then_inc(s, 16)
                else:
                    sp.dma_start(a3(slot[:, 0:2048], 2), rows(a["w_sh_down"][0])).then_inc(s, 16)
                    sp.dma_start(a3(slot[:, 2048:2560], 8), rows(a["w_router"][0])).then_inc(s, 16)

            sp.dma_start(c_in, a["c"][0].rearrange("(p k) -> p k", k=KD)).then_inc(S["c_in"], 16)
            sp.wait_ge(S["ada_zero"], 1)
            sp.dma_start(ADA[0:1, :], a["b_ada"][0:1, :]).then_inc(S["b_in"], 16)
            for g in ITEMS:
                if g == ("A", 6):
                    sp.wait_ge(S["u_rows"], 16 * TT)
                    for s in range(CH):
                        sp.dma_start(UB[0:NC, 512 * (7 - s):512 * (8 - s)],
                                     UD.rearrange("(c s) n -> c s n", s=CH)[:, s, :]).then_inc(S["u_chunks"], 16)
                load(g)
                if g == ("A", 1):
                    sp.dma_start(H[:], a["x"][0].rearrange("(t p) d -> p t d", p=P)).then_inc(S["x_in"], 16)

            def expert(r, blk):
                def src(w):
                    v = a[w][0].rearrange("(b r) k n -> b r k n", r=RING)
                    return v[bass.ds(blk, 1), r].rearrange("b k n -> (b k) n").rearrange("(k p) n -> p k n", p=P)
                sp.dma_start(wgu[r][:, :, 0:ED], src("w_exp_gate")).then_inc(w_in_sem[r], 16)
                sp.dma_start(wgu[r][:, :, ED:2 * ED], src("w_exp_up")).then_inc(w_in_sem[r], 16)
                sp.dma_start(wdn[r], src("w_exp_down")).then_inc(w_in_sem[r], 16)

            sp.wait_ge(S["mixed"], KD)
            expert(0, 0)
            expert(1, 0)
            taken(sp, ("dn", TT - 1, 1))
            expert(2, 0)
            expert(3, 0)
            with sp.Fori(1, NE // RING) as blk:
                for r in range(RING):
                    sp.wait_ge(S["expert_done"], blk * RING + (r - RING + 1))
                    expert(r, blk)

            sp.wait_ge(S["expert_done"], NE - 3)
            sp.wait_ge(S["ov_row"], 16)
            n_ov = sp.value_load(ovrow[0:1, 0:1], min_val=0, max_val=MAXOV)
            with sp.Fori(0, (MAXOV + 1) // 2) as jj:
                for u in range(2):
                    with sp.If(n_ov > jj * 2 + u):
                        e = sp.value_load(ovrow[0:1, bass.ds(jj * 2 + (u + MAXOV + 1), 1)], min_val=0, max_val=NE - 1)
                        if u:
                            sp.wait_ge(S["expert_done"], NE - 2)
                        sp.wait_ge(S["ov_y"], jj * 2 + (u + 1))
                        sp.wait_ge(S["ov_x"], jj * 32 + 16 * (u + 1))

                        def src(w):
                            return a[w][0][bass.ds(e, 1)].rearrange("e k n -> (e k) n").rearrange("(k p) n -> p k n", p=P)
                        sp.dma_start(wgu[u][:, :, 0:ED], src("w_exp_gate")).then_inc(ov_w[u], 16)
                        sp.dma_start(wgu[u][:, :, ED:2 * ED], src("w_exp_up")).then_inc(ov_w[u], 16)
                        sp.dma_start(wdn[u], src("w_exp_down")).then_inc(ov_w[u], 16)

            sp.wait_ge(S["all_added"], 1)
            for t in range(TT):
                sp.dma_start(XT[:, DM * t:DM * (t + 1)], ACC[0][P * t:P * (t + 1), :]).then_inc(sum_in[t], 16)
                sp.dma_start(ut4[:, t], ACC[1][P * t:P * (t + 1), :]).then_inc(sum_in[t], 16)
            for t in range(TT):
                sp.wait_ge(S["final"], t + 1)
                sp.dma_start(out[0, P * t:P * (t + 1), :], H[:, t, :]).then_inc(S["out_done"], 16)
            sp.wait_ge(S["out_done"], 16 * TT)

        @block.gpsimd
        def _(pool):
            n_o = [0]
            E = nc.gpsimd

            def link(ins):
                n_o[0] += 1
                ins.then_inc(S["pool_o"], 1)
                pool.wait_ge(S["pool_o"], n_o[0])

            E.memset(ADA[:], 0.0).then_inc(S["ada_zero"], 1)
            for j, w in enumerate(("ssm_lambda_re", "ssm_lambda_im")):
                for half in range(2):
                    pool.dma_start(lamn[:, P * j + 64 * half:P * j + 64 * half + 64], a[w][0]).then_inc(S["lam_in"], 16)
            pool.dma_start(dtb, a["ssm_log_dt"][0:1, :].broadcast_to((P, G))).then_inc(S["dt_in"], 16)
            for j in range(4):
                for n, pair in enumerate((("ssm_c_re", "ssm_c_im"), ("ssm_c_im", "ssm_c_re"))):
                    for half, w in enumerate(pair):
                        pool.dma_start(cn[:, 2 * j + n, 64 * half:64 * half + 64],
                                       a[w][0, 8 * j:8 * j + 8].rearrange("g h p -> (g h) p")).then_inc(S["ct_in"], 16)
            for dst, pair in ((B1, ("ssm_b_re", "ssm_b_im")), (B2, ("ssm_b_im", "ssm_b_re"))):
                for half, w in enumerate(pair):
                    pool.dma_start(a3(dst, G)[64 * half:64 * half + 64], a[w][0].rearrange("g p h -> p g h")).then_inc(S["bt_in"], 16)
            with nc.allow_non_contiguous_dma(reason="1024 values in all"):
                pool.dma_start(dsk, a["ssm_d"][0].rearrange("(g h) -> h g", h=GH)).then_inc(S["dsk_in"], 16)
                pool.dma_start(bglu, a["ssm_b_glu"][0].rearrange("(m p) -> p m", p=P)).then_inc(S["bglu_in"], 16)

            link(E.memset(ones[:], 1.0))
            E.affine_select(out=sg, in_=ones[:, 0:1], compare_op=ALU.is_gt, fill=-1.0, base=64, pattern=[[0, 1]], channel_multiplier=-1)
            E.affine_select(out=nsg, in_=ones[:, 0:1], compare_op=ALU.is_ge, fill=-1.0, base=-64, pattern=[[0, 1]], channel_multiplier=1)
            E.memset(W3, 0.0)
            E.memset(GC, 0.0)
            E.memset(GS, 0.0)
            E.memset(UB[:, 0:DM], 0.0)
            E.iota(iota[:], [[1, SEQ]], base=0, channel_multiplier=0, allow_small_or_imprecise_dtypes=True)
            E.iota(tokid, [[P, TT]], base=0, channel_multiplier=1, allow_small_or_imprecise_dtypes=True)
            E.iota(dummy, [[1, 1]], base=SEQ, channel_multiplier=1, allow_small_or_imprecise_dtypes=True)
            E.iota(pp1, [[1, 1]], base=1, channel_multiplier=1, allow_small_or_imprecise_dtypes=True)
            link(E.memset(ident[:], 0.0))
            E.affine_select(out=lower[:], in_=ones[:], compare_op=ALU.is_gt, fill=0.0, base=0,
                            pattern=[[1, P]], channel_multiplier=-1)
            E.affine_select(out=ident[:], in_=ident[:], compare_op=ALU.not_equal, fill=1.0, base=0,
                            pattern=[[-1, P]], channel_multiplier=1).then_inc(S["consts"], 1)
            pool.wait_ge(S["consts"], 1)
            for j in range(TT + 1):
                for n in range(2):
                    pool.dma_start(ACC[n][P * j:P * (j + 1), :], UB[:, 0:DM]).then_inc(y_added[n], 16)

            lr, li = lam[:, 0:32], lam[:, 32:64]
            taken(pool, ("lam", 0))
            pool.wait_ge(S["dt_exp"], 1)

            def reduce_angle(ang, n, t):
                link(E.tensor_scalar(n, ang, 1.0 / TWO_PI, MAGIC, ALU.mult, ALU.add))
                link(E.tensor_scalar(n, n, MAGIC, None, ALU.subtract))
                for c in (C1, C2, C3):
                    link(E.tensor_scalar(t, n, c, None, ALU.mult))
                    link(E.tensor_tensor(ang, ang, t, ALU.subtract))

            def sin_cos(ang, n, sin_arg, cos_arg, k):
                link(E.tensor_scalar(cos_arg, ang, math.pi / 2, None, ALU.add))
                link(E.tensor_scalar(n, cos_arg, math.pi, TWO_PI, ALU.is_gt, ALU.mult))
                link(E.tensor_tensor(cos_arg, cos_arg, n, ALU.subtract))
                link(E.tensor_scalar(cos_arg, cos_arg, SIN_MAX, -SIN_MAX, ALU.min, ALU.max))
                E.tensor_scalar(sin_arg, ang, SIN_MAX, -SIN_MAX, ALU.min, ALU.max).then_inc(S["angles"], 1)
                pool.wait_ge(S["sines"], k)

            def tt(o, x, y, op=ALU.mult):
                link(E.tensor_tensor(o, x, y, op))

            tt(m8, lr, dtb)
            tt(th, li, dtb)
            reduce_angle(th, N9[:, 0:32], T512[:, 0:32])
            tau = bc(iota[:, 0:9], G, 2)
            tt(a3(E9, 9), tau, bc(m8, 9, 1))
            tt(a3(A9, 9), tau, bc(th, 9, 1))
            reduce_angle(A9, N9, T512[:, 0:288])
            link(E.tensor_copy(th, A9[:, 256:288]))
            sin_cos(A9, N9, AimS, Are, 1)
            tt(Are, Are, E9)
            tt(AimS, AimS, E9)
            link(E.tensor_copy(m8, E9[:, 256:288]))
            nr, den, fr, fi, t1 = fcol
            are1, aim1 = Are[:, 32:64], AimS[:, 32:64]
            link(E.tensor_scalar(nr, are1, -1.0, None, ALU.add))
            tt(den, lr, lr)
            tt(t1, li, li)
            tt(den, den, t1, ALU.add)
            tt(fr, nr, lr)
            tt(t1, aim1, li)
            tt(fr, fr, t1, ALU.add)
            tt(fi, aim1, lr)
            tt(t1, nr, li)
            tt(fi, fi, t1, ALU.subtract)
            link(E.memset(D0[:, 0:32], -1.0))
            tt(den, den, D0[:, 0:32], ALU.pow)
            tt(fr, fr, den)
            tt(fi, fi, den)
            link(E.tensor_scalar(fi, fi, nsg, None, ALU.mult))
            link(E.tensor_scalar(AimS, AimS, nsg, None, ALU.mult))
            pool.wait_ge(S["bt_in"], 64)
            frb, fib = bc(fr, GH, 2), bc(fi, GH, 2)
            tt(a3(Xb, G), a3(B1, G), frb)
            tt(a3(T512, G), a3(B2, G), fib)
            tt(Xb, Xb, T512, ALU.add)
            tt(a3(Zb, G), a3(B2, G), frb)
            tt(a3(T512, G), a3(B1, G), fib)
            E.tensor_tensor(Zb, Zb, T512, ALU.subtract).then_inc(S["b_ok"], 1)
            pool.wait_ge(S["b_ok"], 1)

            def powers(tab, lo, n, q):
                v = a3(tab, 9)[:, lo:lo + n, QG * q:QG * (q + 1)].rearrange("p t g -> p g t")
                return bc(v, GH, 3)

            def coef(tab, n, q):
                return bc(a3(tab, G)[:, QG * q:QG * (q + 1), :], n, 2)

            def v4(ap):
                return ap.rearrange("p (g t h) -> p g t h", g=QG, h=GH)

            def causal(i):
                pool.wait_ge(S["relu_free"], NH * i)
                d = sc_of[i][:, P * i:P * (i + 1)]
                E.affine_select(out=d, in_=d, compare_op=ALU.is_ge, fill=MASKED, base=0,
                                pattern=[[-1, P]], channel_multiplier=1).then_inc(S["causal"], 1)

            def s5_tables(q):
                if q:
                    pool.wait_ge(S["rotated"], q)
                tt(a3(D0, QG), bc(iota[:, 0:NC], QG, 1), bc(th[:, QG * q:QG * (q + 1)], NC, 2))
                reduce_angle(D0, SIN, COS)
                sin_cos(D0, T512, SIN, COS, 2 + q)
                link(E.tensor_scalar(SIN, SIN, sg, None, ALU.mult))
                link(E.tensor_copy(a3(D0, QG), bc(m8[:, QG * q:QG * (q + 1)], NC, 2)))
                E.memset(a3(D0, QG)[:, :, 0:1], 0.0).then_inc(S["tables"], 1)
                if q:
                    taken(pool, ("y", q - 1, 1))
                tt(v4(BA), coef(Xb, 8, q), powers(Are, 0, 8, q))
                tt(v4(CA[:, 0:1024]), coef(Zb, 8, q), powers(AimS, 0, 8, q))
                E.tensor_tensor(BA, BA, CA[:, 0:1024], ALU.add).then_inc(S["ba_ok"], 1)
                pool.wait_ge(S["ba_ok"], q + 1)
                taken(pool, ("cT", 3))
                tt(v4(CA), coef(X, 9, q), powers(Are, 0, 9, q))
                for lo, n in ((0, 4), (4, 4), (8, 1)):
                    tt(v4(T512[:, 0:QG * n * GH]), coef(Z, n, q), powers(AimS, lo, n, q))
                    last = E.tensor_tensor(v4(CA)[:, :, lo:lo + n], v4(CA)[:, :, lo:lo + n],
                                           v4(T512[:, 0:QG * n * GH]), ALU.subtract)
                    if lo < 8:
                        link(last)
                last.then_inc(S["ca_ok"], 1)
                pool.wait_ge(S["ca_ok"], q + 1)
                tt(v4(W2), coef(Z, 8, q), powers(Are, 1, 8, q))
                for lo in (0, 4):
                    tt(v4(T512), coef(X, 4, q), powers(AimS, lo + 1, 4, q))
                    last = E.tensor_tensor(v4(W2)[:, :, lo:lo + 4], v4(W2)[:, :, lo:lo + 4], v4(T512), ALU.add)
                    if lo == 0:
                        link(last)
                last.then_inc(S["w2_ok"], 1)
                pool.wait_ge(S["k_full"], q + 1)
                for j in range(CH):
                    s = CH - 1 - j
                    pool.dma_start(a3(W3, QG)[GH * j:GH * (j + 1), :, GH * s:P],
                                   a3(K16, QG)[:, :, 0:GH * (CH - s)]).then_inc(S["toeplitz"], 16)
                pool.wait_ge(S["w2_ok"], q + 1)

            s5_tables(0)
            s5_tables(1)
            causal(1)
            causal(2)
            s5_tables(2)
            causal(3)
            s5_tables(3)

            taken(pool, ("y", NQ - 1, 1))
            for i in range(TT):
                last = E.iota(Mb[i], [[1, P * (i + 1)]], base=-P * i, channel_multiplier=-1,
                              allow_small_or_imprecise_dtypes=True)
                if i == 0:
                    link(last)
                    last = E.affine_select(out=Mb[0], in_=Mb[0], compare_op=ALU.is_ge, fill=MASKED, base=0,
                                           pattern=[[-1, P]], channel_multiplier=1)
                last.then_inc(S["dist"], 1)

            for t in range(TT):
                pool.wait_ge(S["u2_tile"], t + 1)
                pool.dma_start(U2D[P * t:P * (t + 1), :], ut4[:, t, :]).then_inc(S["u2_rows"], 16)
            pool.wait_ge(S["u2_rows"], 16 * TT)
            taken(pool, ("u2T", TT - 1, 1))
            pool.dma_start(rbias, a["router_bias"][0:1, :].broadcast_to((P, NE))).then_inc(S["bias_in"], 16)
            E.iota(ovc, [[1, NE], [0, XB]], base=0, channel_multiplier=0, allow_small_or_imprecise_dtypes=True)
            E.iota(ovt, [[0, NE], [P, XB]], base=P, channel_multiplier=0, allow_small_or_imprecise_dtypes=True)
            E.memset(UB[:, 0:TT * NEP * 3], 0.0)
            E.memset(UB[:, 816:816 + TT * NEP], -1.0)
            link(E.memset(scr[:, 1952:2016], 1.0))
            E.affine_select(out=lt8, in_=lt8, compare_op=ALU.is_gt, fill=0.0, base=0,
                            pattern=[[1, 8], [-1, 8]], channel_multiplier=0).then_inc(S["masks"], 1)

            pool.wait_ge(S["ov_list"], 1)
            pool.dma_start(OVD, ovi[0:MAXOV + 1, :]).then_inc(S["ov_out"], 16)
            pool.wait_ge(S["ov_out"], 16)
            with nc.allow_non_contiguous_dma(reason="96 values"):
                pool.dma_start(ovrow[:, 0:3 * (MAXOV + 1)].rearrange("a (c j) -> a c j", c=3), OVD.rearrange("(a j) c -> a c j", a=1)).then_inc(S["ov_row"], 16)

            taken(pool, ("dn", TT - 1, 1))
            E.memset(XT[:, 0:2048], 0.0).then_inc(S["x_zero"], 1)
            pool.wait_ge(S["x_zero"], 1)

            def gather(par, col, s):
                pool.sem_inc(S["pool_turn"], 1)
                E.indirect_dma_start(xg[par], None, U2D, bass.IndirectOffsetOnAxis(idx[:, col:col + 1], 0),
                                     bounds_check=SEQ - 1, oob_is_err=False).then_inc(s, 16)

            def add(par, s):
                pool.sem_inc(S["pool_turn"], 1)
                E.indirect_dma_start(ACC[par], bass.IndirectOffsetOnAxis(adx[:, par:par + 1], 0), ye[par], None,
                                     compute_op=ALU.add, bounds_check=SEQ + P - 1).then_inc(s, 16)

            def add_expert(blk, r):
                e = blk * RING + r
                pool.wait_ge(S["y_out_s"], e + 1)
                pool.wait_ge(S["y_out_v"], e + 1)
                added(pool, blk, r - 2)
                add(r % 2, y_added[r % 2])

            for _ in range(2):
                pool.sem_inc(S["ov_y"], 1)
                pool.sem_inc(S["ov_yo"], 1)
            for e in range(2):
                pool.wait_ge(S["list_out"], e + 1)
                gather(e, e, gathered[e])

            def step(blk, r):
                e = blk * RING + r
                if follows(blk, r, 2):
                    pool.wait_ge(S["list_out"], e + 3)
                    pool.wait_ge(S["x_tr"], e + 1)
                    gather(r % 2, (r + 2) % RING, gathered[r % 2])
                if not is_first(blk, r):
                    add_expert(blk, r - 1)

            over_blocks(step, pool)
            pool.wait_ge(S["ov_idx"], 1)
            gather(0, 0, S["ov_x"])
            add_expert(NE // RING - 1, RING - 1)
            added(pool, NE // RING - 1, RING - 2)
            added(pool, NE // RING - 1, RING - 1)
            for _ in range(2):
                pool.sem_inc(S["ov_go"], 1)

            pool.wait_ge(S["ov_row"], 16)
            n_ov = pool.value_load(ovrow[0:1, 0:1], min_val=0, max_val=MAXOV)
            with pool.Fori(0, (MAXOV + 1) // 2) as jj:
                for u in range(2):
                    j = jj * 2 + u
                    with pool.If(n_ov > j):
                        pool.wait_ge(S["ov_idx"], j + 2)
                        gather(1 - u, 1 - u, S["ov_x"])
                        pool.wait_ge(S["ov_yo"], j * 2 + 4)
                        add(u, S["ov_add"])
                        pool.wait_ge(S["ov_add"], j * 16 + 16)
                        pool.sem_inc(S["ov_go"], 1)
            pool.wait_ge(S["ov_x"], n_ov * 16 + 16)
            pool.sem_inc(S["all_added"], 1)
            for t in range(TT):
                pool.wait_ge(sum_in[t], 32)
                E.tensor_tensor(ut4[:, t], ut4[:, t], XT[:, DM * t:DM * (t + 1)], ALU.add).then_inc(S["sums_joined"], 1)

        @block.scalar
        def _(act):
            A = nc.scalar.activation
            n_o = [0]

            def link(ins):
                n_o[0] += 1
                ins.then_inc(S["scalar_o"], 1)
                act.wait_ge(S["scalar_o"], n_o[0])

            act.dma_start(GB[:], a["norm1_g"][0:1, :].broadcast_to((P, DM))).then_inc(S["norm_in"], 16)
            act.wait_ge(S["c_in"], 16)
            A(csil, c_in, ACT.Silu).then_inc(S["c_silu"], 1)
            act.wait_ge(S["dt_in"], 16)
            A(dtb, dtb, ACT.Exp).then_inc(S["dt_exp"], 1)
            takes(A(lam, done(act, ("lam", 0))[:, 0:64], ACT.Copy), ("lam", 0))
            act.wait_ge(S["x_in"], 16)
            for t in range(TT):
                link(A(UB[:, DM:2 * DM], H[:, t, :], ACT.Square, accum_out=ssq[:, t:t + 1]))
            A(junk1, ssq[:, 3:4], ACT.Copy).then_inc(S["squares"], 1)

            def root(c, count):
                act.wait_ge(S["inverse"], count)
                A(rstd[:, c], rstd[:, c], ACT.Sqrt).then_inc(S["root"], 1)

            act.wait_ge(S["angles"], 1)
            A(E9, E9, ACT.Exp)
            A(AimS, AimS, ACT.Sin)
            A(Are, Are, ACT.Sin).then_inc(S["sines"], 1)

            def out_copy(g, dst, width=512, func=ACT.Copy, view=None):
                b = done(act, g)
                src = b[:, 0:width] if view is None else view(b)
                takes(A(dst, src, func), g)

            def s5_build(q):
                for n in range(2):
                    out_copy(("bT", q, n), W1[:, 512 * n:512 * (n + 1)])

            def phases(q):
                act.wait_ge(S["angles"], 2 + q)
                A(SIN, SIN, ACT.Sin)
                A(COS, COS, ACT.Sin).then_inc(S["sines"], 1)

            def s5_apply(q):
                act.wait_ge(S["toeplitz"], 16 * CH * (q + 1))
                if q == 0:
                    act.wait_ge(S["u_chunks"], 16 * CH)
                c0 = GH * QG * q
                src = UB[0:NC, :].rearrange("c (s n) -> c s n", s=CH)[:, :, c0:c0 + GH * QG]
                A(uperm.rearrange("c (g s h) -> c s g h", g=QG, s=CH), src.rearrange("c s (g h) -> c s g h", g=QG),
                  ACT.Copy).then_inc(S["u_perm"], 1)
                out_copy(("uc", q), uc)
                Yv = UB[0:NC, :].rearrange("c (t g h) -> c g t h", t=CH, h=GH)
                for n in range(2):
                    g0 = QG * q + 4 * n
                    for g in range(4):
                        b = done(act, ("y", q, n))
                        ins = A(Yv[:, g0 + g], b[0:NC, P * g:P * (g + 1)].rearrange("c (t h) -> c t h", h=GH), ACT.Copy)
                    takes(ins, ("y", q, n))

            def indexer(i):
                w = P * (i + 1)
                for h in range(NH):
                    n = NH * (i - 1) + h
                    if n >= 2:
                        act.wait_ge(S["relu_free"], n - 1)
                    out_copy(("idx", i, h), relu[:, n % 2, 0:w], w, ACT.Relu)

            phases(0)
            root(slice(0, TT), 1)
            for t in range(TT):
                for n in range(2):
                    out_copy(("uT", t, n), uT[:, 4 * n:4 * n + 4, P * t:P * (t + 1)], view=lambda b: a3(b[:, :], 4))
            for t in range(TT):
                out_copy(("ssm", t), unat[:, t, :])
                taken(act, ("ssm", t))
                act.dma_start(UD[P * t:P * (t + 1), :], unat[:, t, :]).then_inc(S["u_rows"], 16)
            s5_build(0)
            out_copy(("kiT", 0), kiT[:])
            out_copy(("kT", 0), kT[:])
            out_copy(("vw", 0), vw[:], view=lambda b: a3(b[:, 0:288], 4))
            s5_apply(0)
            act.wait_ge(S["u_rows"], 16 * TT)
            for m in range(4):
                out_copy(("qiT", m), qiT[:, m, :])
            indexer(1)
            phases(1)
            s5_build(1)
            indexer(2)
            s5_apply(1)
            indexer(3)
            phases(2)
            s5_build(2)
            act.wait_ge(S["b_ok"], 1)
            for m in range(4):
                out_copy(("qT", m), qT[:, m, :])
            s5_apply(2)
            phases(3)
            s5_build(3)
            act.wait_ge(S["relu_free"], 3 * NH)
            for d in range(4):
                out_copy(("gs", d), sgb[:, d, :], func=ACT.Sigmoid)
            s5_apply(3)
            for m in range(4):
                out_copy(("yT", m), yT[:, m, :], func=ACT.Gelu_apprx_tanh)
            for d in range(4):
                out_copy(("ga", d), sab[:, d, :], func=ACT.Sigmoid)

            for i in range(TT):
                w = P * (i + 1)

                def prob(h):
                    n = NH * i + h
                    act.wait_ge(S["t_max"], n + 1)
                    A(tb[n % 3][:, 0:w], tb[n % 3][:, 0:w], ACT.Exp, bias=nb[:, n:n + 1], scale=2.0 ** -(h + 1),
                      accum_out=rsum[:, n:n + 1]).then_inc(S["prob"], 1)

                prob(0)
                for h in range(NH):
                    if h + 1 < NH:
                        prob(h + 1)
                    n = NH * i + h
                    if n >= 2:
                        act.wait_ge(S["av_done"], n - 1)
                    out_copy(("pT", i, h), pTb[n % 2][:, 0:w], w)
                out_copy(("yaT", i), yaT[:, :, P * i:P * (i + 1)], view=lambda b: a3(b[:, :], 4))
            act.wait_ge(S["bglu_in"], 16)
            for m in range(4):
                b = done(act, ("glu", m))
                if m >= 2:
                    act.wait_ge(S["y2_ok"], m - 1)
                takes(A(tb[m % 2], b[:], ACT.Sigmoid, bias=bglu[:, m:m + 1]), ("glu", m))
            act.wait_ge(S["mixed"], 4)
            for d in range(4, 8):
                out_copy(("gs", d), sgb[:, d - 4, :], func=ACT.Sigmoid)
            for d in range(4, 8):
                out_copy(("ga", d), sab[:, d - 4, :], func=ACT.Sigmoid)
            act.wait_ge(S["u_tile"], TT)
            act.dma_start(GB[:], a["norm2_g"][0:1, :].broadcast_to((P, DM))).then_inc(S["norm_in"], 16)
            for t in range(TT):
                act.wait_ge(S["h_out"], 4 + t + 1)
                link(A(XT[:, 0:DM], H[:, t, :], ACT.Square, accum_out=ssq[:, t:t + 1]))
            A(junk1, ssq[:, 3:4], ACT.Copy).then_inc(S["squares"], 1)
            root(slice(0, TT), 2)
            for t in range(TT):
                for n in range(2):
                    out_copy(("u2T", t, n), uT[:, 4 * n:4 * n + 4, P * t:P * (t + 1)], view=lambda b: a3(b[:, :], 4))
            act.wait_ge(S["u2_rows"], 16 * TT)
            out_copy(("rt", 0), sct, func=ACT.Sigmoid, view=lambda b: a3(b[:, 0:256], 4))
            for m in range(2):
                out_copy(("sh", m), XT[:, 1024 + 512 * m:1536 + 512 * m], func=ACT.Silu)
            act.wait_ge(S["u2_tile"], TT)
            act.dma_start(GB[:], a["norm_f_g"].rearrange("(a d) -> a d", a=1).broadcast_to((P, DM))).then_inc(S["norm_in"], 16)

            def copy_x(par, tr, count, s):
                act.wait_ge(tr, count)
                A(xgT[par][:, 0:4], a3(ps[1][:, :], 4), ACT.Copy).then_inc(s, 1)

            def silu(gu, count, s):
                act.wait_ge(gu, count)
                A(hg, ps[0][:, 0:ED], ACT.Silu).then_inc(s, 1)

            def result(blk, r):
                e = blk * RING + r
                act.wait_ge(S["expert_done"], e + 1)
                added(act, blk, r - 2)
                A(ye[r % 2][:, 512:1024], ps[7][:, :], ACT.Copy, scale=gat[:, r % RING:r % RING + 1]).then_inc(S["y_out_s"], 1)

            def step(blk, r):
                e = blk * RING + r
                silu(S["gu_done"], e + 1, S["g_silu"])
                if follows(blk, r, 1):
                    copy_x((r + 1) % 2, S["x_tr"], e + 2, S["x_out_s"])
                if not is_first(blk, r):
                    result(blk, r - 1)

            taken(act, ("dn", TT - 1, 1))
            copy_x(0, S["x_tr"], 1, S["x_out_s"])
            over_blocks(step, act)
            result(NE // RING - 1, RING - 1)

            copy_x(0, S["ov_xt"], 1, S["ov_xs"])
            act.wait_ge(S["ov_row"], 16)
            n_ov = act.value_load(ovrow[0:1, 0:1], min_val=0, max_val=MAXOV)
            with act.Fori(0, (MAXOV + 1) // 2) as jj:
                for u in range(2):
                    j = jj * 2 + u
                    with act.If(n_ov > j):
                        silu(S["ov_gu"], j + 1, S["ov_silu"])
                        copy_x(1 - u, S["ov_xt"], j + 2, S["ov_xs"])
                        act.wait_ge(S["ov_y"], j + 3)
                        act.wait_ge(S["ov_go"], j + 1)
                        A(ye[u][:, 512:1024], ps[7][:, :], ACT.Copy, scale=gat[:, u:u + 1]).then_inc(S["ov_yo"], 1)
            for t in range(TT):
                act.wait_ge(S["fin_add"], t + 1)
                A(XT[:, DM * t:DM * (t + 1)], H[:, t, :], ACT.Square, accum_out=ssq[:, t:t + 1]).then_inc(S["fin_sq"], 1)
                root(slice(t, t + 1), 3 + t)

        @block.vector
        def _(dve):
            V = nc.vector
            n_o = [0]

            def link(ins):
                n_o[0] += 1
                ins.then_inc(S["vector_o"], 1)
                dve.wait_ge(S["vector_o"], n_o[0])

            def signal(ins, s, count):
                ins.then_inc(S[s], 1)
                dve.wait_ge(S[s], count)

            def out(ins, g):
                takes(ins, g)
                taken(dve, g)

            dve.wait_ge(S["consts"], 1)
            for j in range(4):
                b = done(dve, ("cT", j))
                V.tensor_scalar(X[:, P * j:P * (j + 1)], b[:, 0:P], sg, None, ALU.mult)
                takes(V.tensor_scalar(Z[:, P * j:P * (j + 1)], b[:, P:2 * P], nsg, None, ALU.mult), ("cT", j))

            dve.wait_ge(S["b_in"], 16)
            dve.wait_ge(S["c_silu"], 1)

            def ada_piece(n):
                slot = a3(arrived(dve, ("A", n)), 2)
                part, j = n // 4, n % 4
                acc = ADA[:, 2048 * part:2048 * (part + 1)]
                for k in range(2):
                    ins = V.scalar_tensor_tensor(acc, slot[:, k], csil[:, 2 * j + k:2 * j + k + 1], acc, ALU.mult, ALU.add)
                    if k == 0:
                        link(ins)
                signal(ins, "ada_sum", n + 1)

            def ada_out(n):
                out(V.tensor_copy(ADA[:, 512 * n:512 * (n + 1)], done(dve, ("ada", n))[:]), ("ada", n))

            def rms_scale(c, count):
                link(V.tensor_scalar(var[:, c], ssq[:, c], 1.0 / DM, EPS, ALU.mult, ALU.add))
                V.reciprocal(rstd[:, c], var[:, c]).then_inc(S["inverse"], 1)
                dve.wait_ge(S["root"], count)
                link(V.tensor_tensor(newt[:, c], rstd[:, c], rstd[:, c], ALU.mult))
                link(V.tensor_tensor(newt[:, c], newt[:, c], var[:, c], ALU.mult))
                link(V.tensor_scalar(newt[:, c], newt[:, c], -0.5, 1.5, ALU.mult, ALU.add))
                link(V.tensor_tensor(rstd[:, c], rstd[:, c], newt[:, c], ALU.mult))

            for n in range(4):
                ada_piece(n)
            for n in range(4):
                ada_out(n)
            dve.wait_ge(S["norm_in"], 16)
            link(V.scalar_tensor_tensor(ADA[:, DM:2 * DM], ADA[:, DM:2 * DM], 1.0, GB[:], ALU.add, ALU.mult))
            dve.wait_ge(S["squares"], 1)
            rms_scale(slice(0, TT), 1)
            for n in range(2):
                dve.wait_ge(y_added[n], ADD0)
            for t in range(TT):
                link(V.scalar_tensor_tensor(ut4[:, t], H[:, t], rstd[:, t:t + 1], ADA[:, DM:2 * DM], ALU.mult, ALU.mult))
                signal(V.tensor_tensor(ut4[:, t], ut4[:, t], ADA[:, 0:DM], ALU.add), "u_tile", t + 1)

            def s5_kernel(q):
                if q:
                    dve.wait_ge(S["toeplitz"], 16 * CH * q)
                for n in range(2):
                    b = done(dve, ("K", q, n))
                    out(V.tensor_copy(K16[:, 512 * n:512 * (n + 1)], b[0:GH, :]), ("K", q, n))
                dve.wait_ge(S["dsk_in"], 16)
                link(V.tensor_tensor(a3(kd, QG), bc(ident[0:GH, 0:GH], QG, 1), bc(dsk[:, QG * q:QG * (q + 1)], GH, 2), ALU.mult))
                d = a3(K16, QG)[:, :, 0:GH]
                V.tensor_tensor(d, d, a3(kd, QG), ALU.add).then_inc(S["k_full"], 1)

            def s5_scan(q):
                dve.wait_ge(S["tables"], q + 1)
                b = done(dve, ("v1", q))
                takes(V.tensor_tensor(Vt, b[:], COS, ALU.mult), ("v1", q))
                b = done(dve, ("v2", q))
                takes(V.tensor_tensor(GV, b[:], SIN, ALU.mult), ("v2", q))
                taken(dve, ("v2", q))
                link(V.tensor_tensor(Vt, Vt, GV, ALU.add))
                link(V.tensor_tensor_scan(GV, D0, Vt, 0.0, ALU.mult, ALU.add))
                g3 = a3(GV, QG)[:, :, 0:NC - 1]
                V.tensor_tensor(a3(GC, QG)[:, :, 1:NC], g3, a3(COS, QG)[:, :, 0:NC - 1], ALU.mult)
                V.tensor_tensor(a3(GS, QG)[:, :, 1:NC], g3, a3(SIN, QG)[:, :, 0:NC - 1], ALU.mult).then_inc(S["rotated"], 1)

            def index_scores(i):
                w = P * (i + 1)
                for h in range(NH):
                    n = NH * (i - 1) + h
                    taken(dve, ("idx", i, h))
                    wcol = wis[:, i, h:h + 1]
                    if h == 0:
                        ins = V.tensor_scalar(sc_of[i], relu[:, n % 2, 0:w], wcol, None, ALU.mult)
                    else:
                        ins = V.scalar_tensor_tensor(sc_of[i], relu[:, n % 2, 0:w], wcol, sc_of[i], ALU.mult, ALU.add)
                    signal(ins, "relu_free", n + 1)

            def top_k(i, r0, r1):
                if r0 == 0:
                    dve.wait_ge(S["causal"], i)
                for _ in range(r0, r1):
                    link(V.max(top8, sc_of[i]))
                    link(V.match_replace(sc_of[i], top8, sc_of[i], TAKEN))

            for n in range(4, 8):
                ada_piece(n)
            s5_kernel(0)
            taken(dve, ("vw", 0))
            link(V.tensor_scalar(wis, vw[:, :, HD:HD + NH], float(NH * 64) ** -0.5, None, ALU.mult))
            s5_scan(0)
            for n in range(8, 12):
                ada_piece(n)
            index_scores(1)
            s5_kernel(1)
            index_scores(2)
            s5_scan(1)
            top_k(1, 0, 16)
            index_scores(3)
            s5_kernel(2)
            top_k(2, 0, 16)
            s5_scan(2)
            s5_kernel(3)
            for n in range(4, 12):
                ada_out(n)
            top_k(3, 0, 8)
            s5_scan(3)
            top_k(3, 8, 16)

            for i in range(1, TT):
                dve.wait_ge(S["dist"], i + 1)
                link(V.tensor_scalar(sc_of[i], sc_of[i], LIM, MASKED, ALU.is_gt, ALU.mult))
                link(V.tensor_tensor(Mb[i], Mb[i], sc_of[i], ALU.add))
            for i in range(TT):
                w = P * (i + 1)
                for h in range(NH):
                    n = NH * i + h
                    if n >= 3:
                        done(dve, ("pT", (n - 3) // NH, (n - 3) % NH))
                    b = done(dve, ("lg", i, h))
                    t = tb[n % 3][:, 0:w]
                    out(V.scalar_tensor_tensor(t, b[:, 0:w], 2.0 ** (h + 1) * HD ** -0.5, Mb[i], ALU.mult, ALU.add), ("lg", i, h))
                    link(V.reduce_max(mx[:, n:n + 1], t, axis=AX.X))
                    V.tensor_scalar(nb[:, n:n + 1], mx[:, n:n + 1], -(2.0 ** -(h + 1)), None, ALU.mult).then_inc(S["t_max"], 1)
                hd = slice(NH * i, NH * (i + 1))
                dve.wait_ge(S["prob"], NH * (i + 1))
                link(V.reciprocal(rinv[:, hd], rsum[:, hd]))
                dve.wait_ge(S["av_done"], NH * (i + 1))
                if i:
                    done(dve, ("yaT", i - 1))
                V.tensor_tensor(a3(yat, NH), a3(ps[6 + i % 2][:, :], NH), bc(rinv[:, hd], HD, 2), ALU.mult).then_inc(S["y_att"], 1)

            for m in range(4):
                taken(dve, ("glu", m))
                done(dve, ("glu", 3))
                V.tensor_tensor(y2T[:, m, :].rearrange("p (c t) -> p t c", t=CH), a3(yT[:, m, :], CH), a3(tb[m % 2], CH),
                                ALU.mult).then_inc(S["y2_ok"], 1)
            for d in range(KD):
                taken(dve, ("ga", d))
                b = done(dve, ("ps", d))
                takes(V.tensor_tensor(mixT[:, d], b[:], sgb[:, d % 4], ALU.mult), ("ps", d))
                b = done(dve, ("pa", d))
                out(V.tensor_tensor(tmpv, b[:], sab[:, d % 4], ALU.mult), ("pa", d))
                signal(V.tensor_tensor(mixT[:, d], mixT[:, d], tmpv, ALU.add), "mixed", d + 1)
            dve.wait_ge(S["norm_in"], 32)
            link(V.scalar_tensor_tensor(ADA[:, 4 * DM:5 * DM], ADA[:, 4 * DM:5 * DM], 1.0, GB[:], ALU.add, ALU.mult))
            for n in range(2):
                for t in range(TT):
                    b = done(dve, ("out", t, n))
                    hh = H[:, t, 512 * n:512 * (n + 1)]
                    out(V.tensor_tensor(tmp2, b[:], ADA[:, 2 * DM + 512 * n:2 * DM + 512 * (n + 1)], ALU.mult), ("out", t, n))
                    signal(V.tensor_tensor(hh, hh, tmp2, ALU.add), "h_out", TT * n + t + 1)
            dve.wait_ge(S["squares"], 2)
            rms_scale(slice(0, TT), 2)
            for t in range(TT):
                link(V.scalar_tensor_tensor(ut4[:, t], H[:, t], rstd[:, t:t + 1], ADA[:, 4 * DM:5 * DM], ALU.mult, ALU.mult))
                signal(V.tensor_tensor(ut4[:, t], ut4[:, t], ADA[:, 3 * DM:4 * DM], ALU.add), "u2_tile", t + 1)

            dve.wait_ge(S["bias_in"], 16)
            dve.wait_ge(S["masks"], 1)
            taken(dve, ("rt", 0))
            link(V.tensor_tensor(bia, sct, bc(rbias, TT, 1), ALU.add))
            b4 = bia.rearrange("p t (g k) -> p t g k", g=NGR)
            for t in range(TT):
                for g in range(NGR):
                    ins = V.max(m2[:, t, g], b4[:, t, g])
            link(ins)
            link(V.tensor_tensor(gsum, m2[:, :, :, 0], m2[:, :, :, 1], ALU.add))
            mine, other = bc(gsum, NGR, 3), bc(gsum, NGR, 2)
            link(V.tensor_tensor(cmp, other, mine, ALU.is_gt))
            link(V.tensor_tensor(cmp2, other, mine, ALU.is_equal))
            link(V.tensor_tensor(cmp2, cmp2, bc(lt8, TT, 1), ALU.mult))
            link(V.tensor_tensor(cmp, cmp, cmp2, ALU.add))
            link(V.tensor_reduce(rank, cmp, axis=AX.X, op=ALU.add))
            link(V.tensor_scalar(gm, rank, float(TG) - 0.5, MASKED, ALU.is_gt, ALU.mult))
            link(V.tensor_tensor(wk.rearrange("p t (g k) -> p t g k", g=NGR), b4, bc(gm, EPG, 3), ALU.add))
            for t in range(TT):
                link(V.max(m2[:, t, 0], wk[:, t]))
                link(V.match_replace(wk[:, t], m2[:, t, 0], wk[:, t], TAKEN))
            signal(V.tensor_scalar(Mm, wk, LIM, None, ALU.is_lt), "slots", 1)
            link(V.tensor_tensor(bia, sct, Mm, ALU.mult))
            link(V.tensor_reduce(gsm, bia, axis=AX.X, op=ALU.add))
            link(V.reciprocal(gsm, gsm))
            link(V.tensor_scalar(gsm, gsm, ROUTED_SCALE, None, ALU.mult))
            link(V.tensor_tensor(RG[:, :, 0:NE, 1], bia, bc(gsm, NE, 2), ALU.mult))
            link(V.tensor_scalar(RG[:, :, 0:NE, 2], Mm, 1.0, None, ALU.mult))
            link(V.tensor_tensor(RG[:, :, 0:NE, 0], Mm, bc(tokid, NE, 2), ALU.mult))

            for m in range(2):
                b = done(dve, ("sh", 2 + m))
                taken(dve, ("sh", m))
                takes(V.tensor_tensor(XT[:, 512 * m:512 * (m + 1)], b[:], XT[:, 1024 + 512 * m:1536 + 512 * m], ALU.mult),
                      ("sh", 2 + m))
            b = done(dve, ("pos", 0))
            out(V.scalar_tensor_tensor(posm[:, :, 0:NE], a3(b[:, 0:TT * NE], TT), 1.0, Mm, ALU.add, ALU.mult), ("pos", 0))
            link(V.tensor_scalar(posm[:, :, 0:NE], posm[:, :, 0:NE], -1.0, None, ALU.add))
            b = done(dve, ("cnt", 0))
            out(V.tensor_copy(cnt, b[:, 0:NE]), ("cnt", 0))
            link(V.tensor_tensor(ovf.rearrange("p (e b) -> p e b", b=XB), bc(cnt, XB, 2), ovt.rearrange("p (e b) -> p e b", b=XB), ALU.is_gt))
            link(V.memset(ovo, 1.0))
            link(V.tensor_tensor_scan(ovr, ovo, ovf, 0.0, ALU.mult, ALU.add))
            link(V.tensor_copy(ovl[:, 0:1], ovr[:, XB * NE - 1:XB * NE]))
            link(V.scalar_tensor_tensor(ovr, ovr, pp1, ovf, ALU.is_equal, ALU.mult))
            link(V.tensor_tensor(ovf, ovr, ovc, ALU.mult))
            link(V.tensor_reduce(ovl[:, 1:2], ovf, axis=AX.X, op=ALU.add))
            link(V.tensor_tensor(ovf, ovr, ovt, ALU.mult))
            link(V.tensor_reduce(ovl[:, 2:3], ovf, axis=AX.X, op=ALU.add))
            V.tensor_copy(ovi[:], ovl[:, 0:3]).then_inc(S["ov_list"], 1)

            for t in range(TT):
                for n in range(2):
                    b = done(dve, ("dn", t, n))
                    hh = H[:, t, 512 * n:512 * (n + 1)]
                    out(V.tensor_tensor(tmp2, b[:], ADA[:, 5 * DM + 512 * n:5 * DM + 512 * (n + 1)], ALU.mult), ("dn", t, n))
                    link(V.tensor_tensor(hh, hh, tmp2, ALU.add))

            def make_hot(par, e, first, s):
                V.tensor_tensor(hot[par], bc(first, TT, 1), posm[:, :, bass.ds(e, 1)].broadcast_to((P, TT, P)), ALU.is_equal)\
                    .then_inc(s, 1)

            def take_list(col, s, count):
                L = ps[5]
                em = empty[col % 2]
                V.tensor_copy(gat[:, col:col + 1], L[:, 1:2])
                V.tensor_scalar(em, L[:, 2:3], -1.0, 1.0, ALU.mult, ALU.add).then_inc(s[0], 1)
                dve.wait_ge(s[0], count)
                V.scalar_tensor_tensor(idx[:, col:col + 1], em, dummy, L[:, 0:1], ALU.mult, ALU.add).then_inc(s[1], 1)

            def copy_x(par, tr, count, s):
                dve.wait_ge(tr, count)
                V.tensor_copy(xgT[par][:, 4:8], a3(ps[2][:, :], 4)).then_inc(s, 1)

            def hidden(si, count, s):
                dve.wait_ge(si, count)
                V.tensor_tensor(hs, hg, ps[0][:, ED:2 * ED], ALU.mult).then_inc(s, 1)

            def hidden_t(ht, count, s):
                dve.wait_ge(ht, count)
                V.tensor_copy(hTe, a3(ps[3][:, 0:2 * P], 2)).then_inc(s, 1)

            first = iota[:, 0:P]
            em_s = (S["empties"], S["list_out"])
            for e in range(2):
                make_hot(e, e, first, S["slot_hot"])
            for e in range(2):
                dve.wait_ge(S["list_done"], e + 1)
                take_list(e, em_s, e + 1)
            copy_x(0, S["x_tr"], 1, S["x_out_v"])
            pv = posm.rearrange("p t (b r) -> p t b r", r=RING)

            def result(blk, r):
                e = blk * RING + r
                dve.wait_ge(S["expert_done"], e + 1)
                added(dve, blk, r - 2)
                V.tensor_copy(adx[:, r % 2:r % 2 + 1], idx[:, r % RING:r % RING + 1])
                V.tensor_scalar(ye[r % 2][:, 0:512], ps[6][:, :], gat[:, r % RING:r % RING + 1], None, ALU.mult)\
                    .then_inc(S["y_out_v"], 1)

            def step(blk, r):
                e = blk * RING + r
                if follows(blk, r, 2):
                    bl, rr = (blk, r + 2) if r < 2 else (blk + 1, r - 2)
                    V.tensor_tensor(hot[r % 2], bc(first, TT, 1),
                                    pv[:, :, bass.ds(bl, 1), rr].broadcast_to((P, TT, P)), ALU.is_equal).then_inc(S["slot_hot"], 1)
                hidden(S["g_silu"], e + 1, S["h_ok"])
                if follows(blk, r, 1):
                    copy_x((r + 1) % 2, S["x_tr"], e + 2, S["x_out_v"])
                if follows(blk, r, 2):
                    dve.wait_ge(S["list_done"], e + 3)
                    take_list((r + 2) % RING, em_s, e + 3)
                if not is_first(blk, r):
                    result(blk, r - 1)
                hidden_t(S["hT_done"], e + 1, S["hT_out"])

            over_blocks(step, dve)

            def more_hot(j, u):
                e = dve.value_load(ovrow[0:1, bass.ds(j + (MAXOV + 1), 1)], min_val=0, max_val=NE - 1)
                slot0 = dve.value_load(ovrow[0:1, bass.ds(j + 2 * (MAXOV + 1), 1)], min_val=0, max_val=XB * P)
                make_hot(u, e, iota[:, bass.ds(slot0, P)], S["ov_hot"])

            dve.wait_ge(S["ov_row"], 16)
            n_ov = dve.value_load(ovrow[0:1, 0:1], min_val=0, max_val=MAXOV)
            more_hot(0, 0)
            dve.wait_ge(S["ov_ldone"], 1)
            take_list(0, (S["ov_em"], S["ov_idx"]), 1)
            result(NE // RING - 1, RING - 1)
            copy_x(0, S["ov_xt"], 1, S["ov_xv"])
            with dve.Fori(0, (MAXOV + 1) // 2) as jj:
                for u in range(2):
                    j = jj * 2 + u
                    with dve.If(n_ov > j):
                        more_hot(j + 1, 1 - u)
                        dve.wait_ge(S["ov_ldone"], j + 2)
                        dve.wait_ge(S["ov_yo"], j * 2 + 2)
                        take_list(1 - u, (S["ov_em"], S["ov_idx"]), j + 2)
                        hidden(S["ov_silu"], j + 1, S["ov_h"])
                        copy_x(1 - u, S["ov_xt"], j + 2, S["ov_xv"])
                        hidden_t(S["ov_ht"], j + 1, S["ov_hts"])
                        dve.wait_ge(S["ov_y"], j + 3)
                        dve.wait_ge(S["ov_go"], j + 1)
                        V.tensor_copy(adx[:, u:u + 1], idx[:, u:u + 1])
                        V.tensor_scalar(ye[u][:, 0:512], ps[6][:, :], gat[:, u:u + 1], None, ALU.mult).then_inc(S["ov_yo"], 1)

            for t in range(TT):
                dve.wait_ge(S["sums_joined"], t + 1)
                x = ut4[:, t]
                link(V.tensor_tensor(x, x, ADA[:, 5 * DM:6 * DM], ALU.mult))
                signal(V.tensor_tensor(H[:, t], H[:, t], x, ALU.add), "fin_add", t + 1)
            dve.wait_ge(S["norm_in"], 48)
            for t in range(TT):
                c = slice(t, t + 1)
                dve.wait_ge(S["fin_sq"], t + 1)
                rms_scale(c, 3 + t)
                V.scalar_tensor_tensor(H[:, t], H[:, t], rstd[:, c], GB[:], ALU.mult, ALU.mult).then_inc(S["final"], 1)

        @block.tensor
        def _(pe):
            mm = nc.tensor.matmul

            def tr(o, i):
                k = i.shape[0]
                return nc.tensor.transpose(o, i, ident[0:k, 0:k])

            def begin(g):
                n = ORDER[g]
                assert n == begun[0], (g, n, begun[0])
                begun[0] += 1
                if n >= NB:
                    taken(pe, AT[n - NB])
                return bank(g)

            def end(ins):
                ins.then_inc(S["group_done"], 1)

            begun = [0]

            def product(g, chunks, rows_=P, cols=512):
                b = begin(g)
                for k, (l, r) in enumerate(chunks):
                    ins = mm(b[0:rows_, 0:cols], l, r, start=(k == 0), stop=(k == len(chunks) - 1))
                return ins

            pe.wait_ge(S["consts"], 1)
            pe.wait_ge(S["lam_in"], 64)
            b = begin(("lam", 0))
            tr(b[:, 0:32], lamn[:, 0:P])
            end(tr(b[:, 32:64], lamn[:, P:2 * P]))
            pe.wait_ge(S["ct_in"], 256)
            for j in range(4):
                b = begin(("cT", j))
                tr(b[:, 0:P], cn[:, 2 * j])
                end(tr(b[:, P:2 * P], cn[:, 2 * j + 1]))

            def ada(n):
                pe.wait_ge(S["ada_sum"], 4 * (n // 4 + 1))
                end(product(("ada", n), [(ones[:], ADA[:, 512 * n:512 * (n + 1)])]))

            def transposed_rows(name):
                for t in range(TT):
                    pe.wait_ge(S["u_tile" if name == "uT" else "u2_tile"], t + 1)
                    for n in range(2):
                        b = begin((name, t, n))
                        for k in range(4):
                            ins = tr(b[:, P * k:P * (k + 1)], ut4[:, t, P * (4 * n + k):P * (4 * n + k + 1)])
                        end(ins)

            def projection_t(name, n, w, c0):
                ins = product((name, n), [(w[:, k, c0:c0 + P], uT[:, k]) for k in range(KD)])
                end(ins)

            def s5_build(q):
                pe.wait_ge(S["ba_ok"], q + 1)
                for n in range(2):
                    b = begin(("bT", q, n))
                    for g in range(4):
                        ins = tr(b[:, P * g:P * (g + 1)], BA[:, P * (4 * n + g):P * (4 * n + g + 1)])
                    end(ins)
                pe.wait_ge(S["ca_ok"], q + 1)
                for n in range(2):
                    b = begin(("K", q, n))
                    for g in range(4):
                        gg = 4 * n + g
                        ins = mm(b[0:GH, P * g:P * (g + 1)], Xb[:, GH * (QG * q + gg):GH * (QG * q + gg + 1)],
                                 CA[:, 144 * gg:144 * gg + P], start=True, stop=True)
                    end(ins)

            def s5_apply(q):
                pe.wait_ge(S["u_perm"], q + 1)
                b = begin(("uc", q))
                for g in range(QG):
                    ins = tr(b[:, NC * g:NC * (g + 1)], uperm[:, P * g:P * (g + 1)])
                end(ins)
                taken(pe, ("bT", q, 1))
                taken(pe, ("uc", q))
                b = begin(("v1", q))
                for g in range(QG):
                    ins = mm(b[:, NC * g:NC * (g + 1)], W1[:, P * g:P * (g + 1)], uc[:, NC * g:NC * (g + 1)], start=True, stop=True)
                end(ins)
                b = begin(("v2", q))
                for g in range(QG):
                    for half in range(2):
                        o = 64 * half
                        ins = mm(b[o:o + 64, NC * g:NC * (g + 1)], W1[:, P * g + 64 - o:P * g + P - o], uc[:, NC * g:NC * (g + 1)],
                                 start=True, stop=True)
                end(ins)
                pe.wait_ge(S["rotated"], q + 1)
                pe.wait_ge(S["w2_ok"], q + 1)
                pe.wait_ge(S["toeplitz"], 16 * CH * (q + 1))
                for n in range(2):
                    b = begin(("y", q, n))
                    for g in range(4):
                        gg = 4 * n + g
                        c, o = slice(NC * gg, NC * (gg + 1)), b[0:NC, P * g:P * (g + 1)]
                        mm(o, GC[:, c], CA[:, 144 * gg + GH:144 * (gg + 1)], start=True, stop=False)
                        mm(o, GS[:, c], W2[:, P * gg:P * (gg + 1)], start=False, stop=False)
                        ins = mm(o, uc[:, c], W3[:, P * gg:P * (gg + 1)], start=False, stop=True)
                    end(ins)

            def indexer(i):
                for h in range(NH):
                    o = 64 * (h % 2)
                    end(product(("idx", i, h), [(qiT[o:o + 64, h // 2, P * i:P * (i + 1)], kiT[o:o + 64, 0:P * (i + 1)])],
                                cols=P * (i + 1)))

            for n in range(4):
                ada(n)
            transposed_rows("uT")
            taken(pe, ("uT", TT - 1, 1))
            w = a3(arrived(pe, ("ssm", 0)), 8)
            for t in range(TT):
                end(product(("ssm", t), [(uT[:, k, P * t:P * (t + 1)], w[:, k]) for k in range(KD)]))
            s5_build(0)
            w = a3(arrived(pe, ("misc", 0))[:, 0:8 * 328], 8)
            projection_t("kiT", 0, w, 0)
            projection_t("kT", 0, w, P)
            b = begin(("vw", 0))
            for t in range(TT):
                for k in range(KD):
                    ins = mm(b[:, 72 * t:72 * (t + 1)], uT[:, k, P * t:P * (t + 1)], w[:, k, 256:328], start=(k == 0), stop=(k == KD - 1))
            end(ins)
            s5_apply(0)
            w = a3(arrived(pe, ("qi", 0)), 8)
            for m in range(4):
                projection_t("qiT", m, w, P * m)
            taken(pe, ("qiT", 3))
            indexer(1)
            s5_build(1)
            indexer(2)
            s5_apply(1)
            indexer(3)
            s5_build(2)
            w = a3(arrived(pe, ("q", 0)), 8)
            for m in range(4):
                projection_t("qT", m, w, P * m)
            s5_apply(2)
            s5_build(3)
            for n in range(4, 12):
                ada(n)

            def gates(name, half):
                w = a3(arrived(pe, (name, half)), 8)
                for d in range(4):
                    projection_t(name, 4 * half + d, w, P * d)

            gates("gs", 0)
            s5_apply(3)
            taken(pe, ("y", NQ - 1, 1))
            yv = UB[0:NC, :].rearrange("c (t n) -> c t n", t=CH)
            for m in range(4):
                b = begin(("yT", m))
                for t in range(CH):
                    ins = tr(b[:, NC * t:NC * (t + 1)], yv[:, t, P * m:P * (m + 1)])
                end(ins)
            gates("ga", 0)
            taken(pe, ("qT", 3))

            for i in range(TT):
                w_ = P * (i + 1)

                def logits(h):
                    o = 64 * (h % 2)
                    end(product(("lg", i, h), [(qT[o:o + 64, h // 2, P * i:P * (i + 1)], kT[o:o + 64, 0:w_])], cols=w_))

                def values(h):
                    taken(pe, ("pT", i, h))
                    n = NH * i + h
                    for s in range(i + 1):
                        ins = mm(ps[6 + i % 2][:, HD * h:HD * (h + 1)], pTb[n % 2][:, P * s:P * (s + 1)], vw[:, s, 0:HD],
                                 start=(s == 0), stop=(s == i))
                    ins.then_inc(S["av_done"], 1)

                logits(0)
                logits(1)
                if i >= 2:
                    pe.wait_ge(S["y_att"], i - 1)
                for h in range(NH):
                    if h + 2 < NH:
                        logits(h + 2)
                    n = NH * i + h
                    pe.wait_ge(S["prob"], n + 1)
                    b = begin(("pT", i, h))
                    for s in range(i + 1):
                        ins = tr(b[:, P * s:P * (s + 1)], tb[n % 3][:, P * s:P * (s + 1)])
                    end(ins)
                    if h:
                        values(h - 1)
                values(NH - 1)
                pe.wait_ge(S["y_att"], i + 1)
                b = begin(("yaT", i))
                for m in range(4):
                    ins = tr(b[:, P * m:P * (m + 1)], yat[:, P * m:P * (m + 1)])
                end(ins)

            taken(pe, ("yT", 3))
            w = a3(arrived(pe, ("glu", 0))[:, 0:2048], 4)
            for m in range(4):
                end(product(("glu", m), [(w[:, k, P * m:P * (m + 1)], yT[:, k]) for k in range(4)]))

            def branches(half):
                wp = arrived(pe, ("pp", half))
                for d in range(4 * half, 4 * half + 4):
                    for name, y, o in (("ps", y2T, 0), ("pa", yaT, 2048)):
                        w = a3(wp[:, o:o + 2048], 4)
                        end(product((name, d), [(w[:, k, P * (d % 4):P * (d % 4 + 1)], y[:, k]) for k in range(4)]))

            pe.wait_ge(S["y2_ok"], 4)
            taken(pe, ("yaT", 3))
            branches(0)
            gates("gs", 1)
            gates("ga", 1)
            branches(1)
            pe.wait_ge(S["mixed"], KD)
            for n in range(2):
                w = a3(arrived(pe, ("out", n)), 8)
                for t in range(TT):
                    end(product(("out", t, n), [(mixT[:, k, P * t:P * (t + 1)], w[:, k]) for k in range(KD)]))
            transposed_rows("u2T")
            taken(pe, ("u2T", TT - 1, 1))
            wd = arrived(pe, ("shd", 0))
            wr = a3(wd[:, 2048:2560], 8)
            b = begin(("rt", 0))
            for t in range(TT):
                for k in range(KD):
                    ins = mm(b[:, NE * t:NE * (t + 1)], uT[:, k, P * t:P * (t + 1)], wr[:, k], start=(k == 0), stop=(k == KD - 1))
            end(ins)
            w = a3(arrived(pe, ("sh", 0)), 8)
            for m in range(4):
                projection_t("sh", m, w, P * m)
            pe.wait_ge(S["slots"], 1)
            b = begin(("pos", 0))
            for t in range(TT):
                for s in range(t + 1):
                    ins = mm(b[:, NE * t:NE * (t + 1)], (ones if s < t else lower)[:], Mm[:, s], start=(s == 0), stop=(s == t))
            end(ins)
            end(product(("cnt", 0), [(ones[:], Mm[:, s]) for s in range(TT)], cols=NE))
            taken(pe, ("sh", 3))
            wv = a3(wd[:, 0:2048], 2)
            for t in range(TT):
                for n in range(2):
                    end(product(("dn", t, n), [(XT[:, 512 * k + P * t:512 * k + P * (t + 1)], wv[:, k, 512 * n:512 * (n + 1)]) for k in range(2)]))
            assert begun[0] == len(ORDER)

            def make_list(par, rhs, s):
                for t in range(TT):
                    ins = mm(ps[5][:, 0:3], hot[par][:, t], rhs(t), start=(t == 0), stop=(t == TT - 1))
                ins.then_inc(s, 1)

            def turn_x(par, s):
                for k in range(KD):
                    ins = tr(ps[1 + k // 4][:, P * (k % 4):P * (k % 4 + 1)], xg[par][:, P * k:P * (k + 1)])
                ins.then_inc(s, 1)

            def gate_up(par, r, s):
                for k in range(KD):
                    ins = mm(ps[0][:, :], xgT[par][:, k], wgu[r][:, k], start=(k == 0), stop=(k == KD - 1))
                ins.then_inc(s, 1)

            def turn_h(s):
                for k in range(2):
                    ins = tr(ps[3][:, P * k:P * (k + 1)], hs[:, P * k:P * (k + 1)])
                ins.then_inc(s, 1)

            def down(r, s):
                for n in range(2):
                    for k in range(2):
                        ins = mm(ps[6 + n][:, :], hTe[:, k], wdn[r][:, k, 512 * n:512 * (n + 1)], start=(k == 0), stop=(k == 1))
                ins.then_inc(s, 1)

            taken(pe, ("dn", TT - 1, 1))
            for e in range(2):
                pe.wait_ge(S["slot_hot"], e + 1)
                if e:
                    pe.wait_ge(S["list_out"], e)
                make_list(e, lambda t: RG[:, t, e, :], S["list_done"])
            pe.wait_ge(gathered[0], 16)
            turn_x(0, S["x_tr"])
            rgv = UB[:, 0:TT * NEP * 3].rearrange("p (t b r c) -> p t b r c", t=TT, r=RING, c=3)

            def down_expert(blk, r):
                e = blk * RING + r
                pe.wait_ge(S["hT_out"], e + 1)
                if r > 0 or not isinstance(blk, int) or blk > 0:
                    pe.wait_ge(S["y_out_s"], e)
                    pe.wait_ge(S["y_out_v"], e)
                down(r % RING, S["expert_done"])

            def step(blk, r):
                e = blk * RING + r
                pe.wait_ge(w_in_sem[r], blk * 48 + 48)
                pe.wait_ge(S["x_out_s"], e + 1)
                pe.wait_ge(S["x_out_v"], e + 1)
                gate_up(r % 2, r, S["gu_done"])
                if follows(blk, r, 1):
                    pe.wait_ge(gathered[(r + 1) % 2], blk * 32 + 16 * ((r + 1) // 2 + 1))
                    turn_x((r + 1) % 2, S["x_tr"])
                if follows(blk, r, 2):
                    pe.wait_ge(S["slot_hot"], e + 3)
                    pe.wait_ge(S["list_out"], e + 2)
                    bl, rr = (blk, r + 2) if r < 2 else (blk + 1, r - 2)
                    make_list(r % 2, lambda t: rgv[:, t, bass.ds(bl, 1), rr, :].rearrange("p b c -> p (b c)"), S["list_done"])
                if not is_first(blk, r):
                    down_expert(blk, r - 1)
                pe.wait_ge(S["h_ok"], e + 1)
                turn_h(S["hT_done"])

            over_blocks(step, pe)

            def more_list(j, u):
                e = pe.value_load(ovrow[0:1, bass.ds(j + (MAXOV + 1), 1)], min_val=0, max_val=NE - 1)
                pe.wait_ge(S["ov_hot"], j + 1)
                make_list(u, lambda t: RG[:, t, bass.ds(e, 1), :].rearrange("p e c -> p (e c)"), S["ov_ldone"])

            pe.wait_ge(S["ov_row"], 16)
            n_ov = pe.value_load(ovrow[0:1, 0:1], min_val=0, max_val=MAXOV)
            more_list(0, 0)
            down_expert(NE // RING - 1, RING - 1)
            pe.wait_ge(S["ov_x"], 16)
            turn_x(0, S["ov_xt"])
            with pe.Fori(0, (MAXOV + 1) // 2) as jj:
                for u in range(2):
                    j = jj * 2 + u
                    with pe.If(n_ov > j):
                        more_list(j + 1, 1 - u)
                        pe.wait_ge(S["ov_xs"], j + 1)
                        pe.wait_ge(S["ov_xv"], j + 1)
                        pe.wait_ge(ov_w[u], jj * 48 + 48)
                        gate_up(u, u, S["ov_gu"])
                        pe.wait_ge(S["ov_x"], j * 16 + 32)
                        turn_x(1 - u, S["ov_xt"])
                        pe.wait_ge(S["ov_h"], j + 1)
                        turn_h(S["ov_ht"])
                        pe.wait_ge(S["ov_hts"], j + 1)
                        pe.wait_ge(S["ov_yo"], j * 2 + 2)
                        down(u, S["ov_y"])


INPUTS = ["x", "c", "w_ada", "b_ada", "norm1_g", "w_in", "ssm_lambda_re", "ssm_lambda_im", "ssm_log_dt", "ssm_b_re",
          "ssm_b_im", "ssm_c_re", "ssm_c_im", "ssm_d", "ssm_w_glu", "ssm_b_glu", "w_proj_ssm", "w_proj_attn", "w_out",
          "norm2_g", "w_router", "router_bias", "w_exp_gate", "w_exp_up", "w_exp_down", "w_sh_gate", "w_sh_up",
          "w_sh_down", "norm_f_g"]


def kernel(**inputs):
    import numpy as np
    import concourse.bacc as bacc
    from concourse.bass_utils import run_bass_kernel_spmd

    nc = bacc.Bacc("TRN2", target_bir_lowering=False, num_devices=1)
    arrays, aps = {}, {}
    for name in INPUTS:
        v = np.ascontiguousarray(inputs[name])
        arrays[f"in_{name}"] = v
        aps[name] = nc.dram_tensor(f"in_{name}", v.shape, mybir.dt.from_np(v.dtype), kind="ExternalInput").ap()
    out = nc.dram_tensor("out_dram", (1, SEQ, DM), F32, kind="ExternalOutput").ap()
    build(nc, aps, out)
    r = run_bass_kernel_spmd(nc, [arrays], core_ids=[0])
    return r.results[0]["out_dram"]
```

```python
import math
from contextlib import ExitStack

import concourse.bass as bass
from concourse import mybir

F32 = mybir.dt.float32
I32 = mybir.dt.int32
BF16 = mybir.dt.bfloat16
ALU = mybir.AluOpType
ACT = mybir.ActivationFunctionType
AX = mybir.AxisListType

P = 128
SEQ, DM = 512, 1024
TT, KD = SEQ // P, DM // P
G, GH, NS = 32, 16, 64
SW = G * GH
CH = 8
NC = SEQ // CH
NQ, QG = 4, G // 4
NH, HD = 8, 64
TOPK = min(256, SEQ // 4)
NE, EK, NGR, TG, ED = 64, 8, 8, 4, 256
EPG = NE // NGR
EPS = 1e-6
ROUTED_SCALE = 2.5
MASKED, TAKEN, LIM = -1.0e30, -3.0e38, -2.0e38
MAGIC = 12582912.0
TWO_PI = 2 * math.pi
C1 = 6.28125
C2 = 1.9350051879882812e-03
C3 = TWO_PI - C1 - C2
SIN_MAX = 3.1415925
NB = 6
RING = 4
NEP = NE + RING
RC = 5
MAXOV = SEQ * EK // (P + 1)
XB = SEQ // P - 1
O_SSM, O_Q, O_K, O_V, O_QI, O_KI, O_WI, O_GS, O_GA = 0, 512, 1024, 1088, 1152, 1664, 1728, 1736, 2760


FILL = {(0, 1): ("ga", 0), (0, 5): ("ga", 1), (1, 1): ("ga", 2), (1, 5): ("ga", 3),
        (2, 2): ("gs", 4), (2, 5): ("gs", 5), (3, 0): ("gs", 6), (3, 3): ("gs", 7)}


def groups_in_order():
    def s5_build(q):
        return [("bT", q, n) for n in range(2)] + [("K", q, n) for n in range(2)]

    def s5_apply(q):
        return [("uc", q), ("v1", q), ("v2", q), ("gs", q)] + [("y", q, n) for n in range(2)]

    o = [("lam", 0)] + [("uT", t, n) for t in range(TT) for n in range(2)] + [("mod", 0)]
    o += [("ssm", t) for t in range(TT)] + [("cT", j) for j in range(4)]
    o += [("kkT", 0), ("vwT", 0), ("vw", 0)] + [("qiT", m) for m in range(4)]
    o += [("idx", 1, h) for h in range(NH)] + s5_build(0)
    o += [("idx", 2, h) for h in range(NH)] + s5_apply(0) + s5_build(1)
    o += [("idx", 3, h) for h in range(NH)] + s5_apply(1) + s5_build(2)
    o += s5_apply(2) + s5_build(3) + s5_apply(3)
    o += [("qT", m) for m in range(4)] + [("yT", m) for m in range(4)]
    for i in range(TT):
        o += [("lg", i, 0), ("lg", i, 1)]
        for h in range(NH):
            if h + 2 < NH:
                o.append(("lg", i, h + 2))
            o.append(("pT", i, h))
            if (i, h) in FILL:
                o.append(FILL[i, h])
            if i and h == 1:
                o.append(("yaT", i - 1))
    o += [("glu", m) for m in range(4)] + [("yaT", TT - 1)] + [("ada", n) for n in range(4, 12)]
    o += [(n, d) for d in range(4) for n in ("ps", "pa")]
    o += [("ga", d) for d in range(4, 8)]
    o += [(n, d) for d in range(4, 8) for n in ("ps", "pa")]
    for t in range(TT + 2):
        o += [("out", t, n) for n in range(2) if t < TT] + [("u2T", t - 2, n) for n in range(2) if t >= 2]
    o += [("rt", 0), ("rtT", 0)] + [("sh", m) for m in range(4)] + [("pos", 0), ("cnt", 0)]
    o += [("dn", t, n) for t in range(TT) for n in range(2)]
    return o


BY_VECTOR = {"cT", "K", "mod", "ada", "v1", "v2", "lg", "ps", "pa", "out", "pos", "cnt", "dn"}
ORDER = {g: n for n, g in enumerate(groups_in_order())}
TAKEN_OUT = {}
for _g in ORDER:
    _v = _g[0] in BY_VECTOR or _g in (("sh", 2), ("sh", 3))
    TAKEN_OUT[_g] = (_v, 1 + sum(1 for v, _ in TAKEN_OUT.values() if v == _v))
AT = {n: g for g, n in ORDER.items()}


def stream_items():
    o = [("A", n) for n in range(4)] + [("ssm", 0), ("misc", 0), ("A", 4), ("qi", 0), ("gs", 0), ("A", 5)]
    o += [("A", 6), ("q", 0), ("A", 7), ("ga", 0), ("A", 8), ("A", 9), ("gs", 1)]
    o += [("A", 10), ("A", 11), ("glu", 0), ("pp", 0), ("ga", 1), ("pp", 1)]
    o += [("out", 0), ("out", 1), ("sh", 0), ("shd", 0)]
    return o


ITEMS = {g: n for n, g in enumerate(stream_items())}
LAST_USE = {("ssm", 0): ("ssm", 3), ("misc", 0): ("vwT", 0), ("qi", 0): ("qiT", 3), ("q", 0): ("qT", 3),
            ("glu", 0): ("glu", 3), ("out", 0): ("out", 3, 0), ("out", 1): ("out", 3, 1), ("sh", 0): ("sh", 3)}
LAST_USE.update({(_n, _h): (_n if _n != "pp" else "pa", 4 * _h + 3) for _n in ("gs", "ga", "pp") for _h in range(2)})
DMAS = {"misc": 3, "pp": 2, "sh": 2, "shd": 2}


def a3(ap, n):
    return ap.rearrange("p (a b) -> p a b", a=n)


def build(nc, a, out):
    U2D = nc.dram_tensor("u2_rows", (SEQ, DM), F32, kind="Internal").ap()
    ACC = [nc.dram_tensor(f"expert_sum{n}", (SEQ, DM), F32, kind="Internal").ap() for n in range(2)]
    OVD = nc.dram_tensor("more_blocks", (MAXOV + 1, 3), I32, kind="Internal").ap()
    UD = nc.dram_tensor("u_ssm_rows", (SEQ, SW), F32, kind="Internal").ap()
    ctx = ExitStack()
    with ctx:
        def sb(name, shape, dt=F32):
            return ctx.enter_context(nc.sbuf_tensor(name, shape, dt))

        ring = sb("ring", [P, RING * 6144])
        strm = [ring[:, 4096 * s:4096 * (s + 1)] for s in range(3)]
        work = ring[:, 3 * 4096:RING * 6144]
        H = sb("H", [P, TT, DM])
        ADA = sb("ADA", [P, 6 * DM])
        uTs = sb("uTs", [P, KD * SEQ])
        uT = a3(uTs[:, :], KD)
        XT = sb("XT", [P, TT * DM])
        qT, qiT = a3(XT[:, 0:2048], 4), a3(XT[:, 2048:4096], 4)
        unat = a3(XT[:, 2048:4096], 4)
        yT, y2T = qiT, qT
        UB = sb("UB", [P, 4096])
        ut4 = a3(UB[:, :], TT)
        mixT = a3(UB[:, :], KD)
        vwT = ADA[0:72, 0:512]
        scT64 = ADA[0:NE, 1024:1536]
        u2t4 = a3(XT[:, :], TT)
        kT = sb("kT", [P, SEQ])
        kiT = sb("kiT", [P, SEQ])
        vw = sb("vw", [P, TT, 72])
        GB = sb("GB", [P, DM])
        ident = sb("ident", [P, P])
        ones = sb("ones", [P, P])
        lower = sb("lower", [P, P])
        iota = sb("iota", [P, SEQ])
        sm = sb("sm", [P, 432])
        csil, c_in = sm[:, 0:8], sm[:, 8:16]
        ssq, rstd = sm[:, 16:20], sm[:, 20:24]
        sg, nsg = sm[:, 24:25], sm[:, 25:26]
        bglu = sm[:, 28:32]
        shT, scT, g1T = sm[:, 252:260], sm[:, 260:268], sm[:, 268:276]
        var, newt = sm[:, 244:248], sm[:, 248:252]
        wis = sm[:, 32:64].rearrange("p (t h) -> p t h", t=TT)
        mx, nb, rsum, rinv = sm[:, 64:96], sm[:, 96:128], sm[:, 128:160], sm[:, 160:192]
        tokp, tokt = sm[:, 192:196], sm[:, 276:280]
        pp1 = sm[:, 197:198]
        top8 = sm[:, 200:208]
        dsk = sm[0:GH, 208:240]
        junk1 = sm[:, 240:241]
        kd = sm[0:GH, 300:428]
        score = sb("score", [P, 1152])
        sc_of = {1: score[:, 0:256], 2: score[:, 256:640], 3: score[:, 640:1152]}
        relu = a3(GB[:, :], 2)
        K16s = sb("K16s", [P, 1024])
        K16 = K16s[64:64 + GH, :]
        uperm = K16s[0:NC, :]
        lamn = K16s[0:G, 0:256]
        at = [0]

        def take(n):
            at[0] += n
            assert at[0] <= 12288
            return work[:, at[0] - n:at[0]]

        BA, W1, W2, W3 = take(1024), take(1024), take(1024), take(1024)
        CAb = [take(1152), XT[:, 512:1664]]
        uc, Vt = take(512), XT[:, 0:512]
        COS, SIN = take(512), take(512)
        Xb, Zb, X, Z = take(512), take(512), take(512), take(512)
        T512, D0, GV, GC, GS = take(512), take(512), take(512), take(512), take(512)
        Are, AimS = take(9 * G), take(9 * G)
        lam, dtb, th, m8 = take(64), take(32), take(32), take(32)
        E9, A9, N9 = score[:, 0:288], score[:, 288:576], score[:, 576:864]
        fcol = [score[:, 864 + 32 * n:896 + 32 * n] for n in range(5)]
        cn = a3(XT[:, 0:1024], 8)
        B1, B2 = XT[:, 1024:1536], XT[:, 1536:2048]
        Mb = [work[:, 0:128], work[:, 128:384], work[:, 384:768], work[:, 768:1280]]
        tb = [work[:, 1280 + 512 * n:1792 + 512 * n] for n in range(3)]
        pTb = [work[:, 2816 + 512 * n:3328 + 512 * n] for n in range(2)]
        yat = work[:, 3840:4352]
        yaT = a3(work[:, 4352:6400], 4)
        sab = a3(work[:, 6400:8448], 4)
        tmpv = work[:, 8448:8960]
        sgb2 = a3(work[:, 8960:11008], 4)
        tmp2 = ADA[:, 0:512]
        sgb = a3(ADA[:, 0:2048], 4)
        ps = [ctx.enter_context(nc.psum_tensor(f"ps{b}", [P, 512], F32)) for b in range(8)]

        S = {}
        for n in """x_in c_in norm_in lam_in ct_in bt_in dt_in dsk_in bglu_in bias_in g1_in consts ada_zero
                zeros acc_zero scan_zero c_silu dt_exp ada_sum squares inverse root rstd_ok u_tile modulation u_ok_v u_ok_s
                angles sines b_ok ba_ok ca_ok w2_ok phase_args phases toeplitz u_rows u_chunks u_perm rotated
                relu_free causal dist t_max prob av_done y_att gates_ok y2_ok mixed h_out
                u2_tile u2_rows masks slots part_rows pool_turn
                group_done out_scalar out_vector vector_o scalar_o pool_o
                x_zero slot_hot list_done list_out x_tr x_out_s x_out_v gu_done g_silu h_ok hT_done hT_out expert_done
                y_out_s y_out_v ov_list ov_out ov_row ov_em ov_go ov_hot ov_ldone ov_idx ov_x ov_xt ov_xs ov_xv ov_gu
                ov_silu ov_h ov_ht ov_hts ov_y ov_yo ov_add all_added sums_joined fin_add fin_sq final out_done""".split():
            S[n] = ctx.enter_context(nc.semaphore(n))
        y_added = [ctx.enter_context(nc.semaphore(f"y_added{n}")) for n in range(2)]
        ov_w = [ctx.enter_context(nc.semaphore(f"ov_weights{n}")) for n in range(2)]
        gathered = [ctx.enter_context(nc.semaphore(f"gathered{n}")) for n in range(2)]
        b_in = [ctx.enter_context(nc.semaphore(f"b_in{n}")) for n in range(2)]
        sum_in = [ctx.enter_context(nc.semaphore(f"sum_in{t}")) for t in range(TT)]
        s_in = [ctx.enter_context(nc.semaphore(f"stream_in{s}")) for s in range(3)]
        w_in_sem = [ctx.enter_context(nc.semaphore(f"expert_in{s}")) for s in range(RING)]

        def bank(g):
            return ps[ORDER[g] % NB]

        def done(eng, g):
            eng.wait_ge(S["group_done"], ORDER[g] + 1)
            return bank(g)

        def taken(eng, g):
            v, n = TAKEN_OUT[g]
            eng.wait_ge(S["out_vector" if v else "out_scalar"], n)

        def takes(ins, g):
            return ins.then_inc(S["out_vector" if TAKEN_OUT[g][0] else "out_scalar"], 1)

        in_value, n_before = {}, [0, 0, 0]
        for g, n in ITEMS.items():
            n_before[n % 3] += 16 * DMAS.get(g[0], 1)
            in_value[g] = n_before[n % 3]

        def arrived(eng, g):
            n = ITEMS[g]
            eng.wait_ge(s_in[n % 3], in_value[g])
            return strm[n % 3]

        def unused(eng, g):
            if g[0] == "A":
                eng.wait_ge(S["ada_sum"], g[1] + 1)
            else:
                done(eng, LAST_USE[g])

        def bc(ap, n, axis):
            shape = list(ap.shape)
            return ap.unsqueeze(axis).broadcast_to(shape[:axis] + [n] + shape[axis:])

        win_k = a["w_in"][0].rearrange("(k p) n -> p k n", p=P)
        wada_k = a["w_ada"][0].rearrange("(p k) n -> p k n", k=KD)

        def rows(w):
            return w.rearrange("(k p) n -> p k n", p=P)

        slot_of = [2, 3, 0, 1]
        wg, wu, wdn = ([ring[:, 6144 * s + 2048 * n:6144 * s + 2048 * (n + 1)] for s in slot_of] for n in range(3))
        wgu = [ring[:, 6144 * s:6144 * s + 4096].rearrange("p (j k n) -> p k j n", j=2, k=KD) for s in slot_of]
        xg = [XT[:, 1024 * n:1024 * (n + 1)] for n in range(2)]
        xgT = [a3(XT[:, 2048 + 1024 * n:3072 + 1024 * n], KD) for n in range(2)]
        ye = [uTs[:, 1024 * n:1024 * (n + 1)] for n in range(2)]
        hot = [a3(uTs[:, 2048 + 256 * n:2304 + 256 * n].bitcast(BF16), TT) for n in range(2)]
        hs, hg = uTs[:, 3072:3328], uTs[:, 3328:3584]
        hTe = a3(uTs[:, 3584:3840], 2)
        idx = sb("idx", [P, RING], I32)
        adx = sb("adx", [P, 2], I32)
        gat = sb("gat", [P, RING])
        part_row = [sm[:, 280 + n:281 + n] for n in range(2)]
        RGs = UB[:, 0:TT * NEP * RC // 2].bitcast(BF16)
        RG = RGs.rearrange("p (t e c) -> p t e c", t=TT, c=RC)
        r1, r2 = a3(UB[:, 1088 + 1376:1088 + 1632], TT), a3(UB[:, 1088 + 1632:1088 + 1888], TT)
        posm = UB[:, 816:816 + TT * NEP].rearrange("p (t e) -> p t e", t=TT)
        scr = UB[:, 1088:4096]
        sct, bia, wk, Mm = (a3(scr[:, 256 * n:256 * (n + 1)], TT) for n in range(4))
        m2 = scr[:, 1024:1280].rearrange("p (t g k) -> p t g k", t=TT, g=NGR)
        gsum, rank, gm = (a3(scr[:, 1280 + 32 * n:1312 + 32 * n], TT) for n in range(3))
        cmp = scr[:, 1376:1632].rearrange("p (t g k) -> p t g k", t=TT, g=NGR)
        cmp2 = scr[:, 1632:1888].rearrange("p (t g k) -> p t g k", t=TT, g=NGR)
        rbias = scr[:, 1888:1952]
        lt8 = scr[:, 1952:2016].rearrange("p (a b) -> p a b", a=8)
        ovf, ovr, ovc, ovt = (scr[:, 2016 + 192 * n:2208 + 192 * n] for n in range(4))
        ovo = scr[:, 1376:1568]
        cnt, ovl = scr[:, 2784:2848], scr[:, 2848:2852]
        gsm = scr[:, 2852:2856]
        ovrow = sb("ovrow", [1, 3 * (MAXOV + 1) + 1], I32)
        ovi = sb("ovi", [P, 3], I32)
        assert MAXOV + 1 <= 32
        OVG = (MAXOV + 1) // 4

        def added(eng, blk, r):
            if not isinstance(blk, int) or RING * blk + r >= 0:
                eng.wait_ge(y_added[r % 2], blk * (8 * RING) + 16 * (r // 2 + 1))

        def over_blocks(step, eng):
            for r in range(RING):
                step(0, r)
            with eng.Fori(1, NE // RING - 1) as blk:
                for r in range(RING):
                    step(blk, r)
            for r in range(RING):
                step(NE // RING - 1, r)

        def is_first(blk, r):
            return isinstance(blk, int) and RING * blk + r == 0

        def follows(blk, r, n):
            return not isinstance(blk, int) or RING * blk + r + n < NE

        block = ctx.enter_context(nc.Block())

        def reduce_angle(E, link, ang, n, t):
            link(E.tensor_scalar(n, ang, 1.0 / TWO_PI, MAGIC, ALU.mult, ALU.add))
            link(E.tensor_scalar(n, n, MAGIC, None, ALU.subtract))
            for c in (C1, C2, C3):
                link(E.tensor_scalar(t, n, c, None, ALU.mult))
                link(E.tensor_tensor(ang, ang, t, ALU.subtract))

        def sin_cos_args(E, link, ang, n, sin_arg, cos_arg):
            link(E.tensor_scalar(cos_arg, ang, math.pi / 2, None, ALU.add))
            link(E.tensor_scalar(n, cos_arg, math.pi, TWO_PI, ALU.is_gt, ALU.mult))
            link(E.tensor_tensor(cos_arg, cos_arg, n, ALU.subtract))
            link(E.tensor_scalar(cos_arg, cos_arg, SIN_MAX, -SIN_MAX, ALU.min, ALU.max))
            return E.tensor_scalar(sin_arg, ang, SIN_MAX, -SIN_MAX, ALU.min, ALU.max)

        @block.sync
        def _(sp):
            def load(g):
                n = ITEMS[g]
                if n >= 3:
                    unused(sp, stream_items()[n - 3])
                slot, s, k = strm[n % 3], s_in[n % 3], g[0]
                if k == "A":
                    part, j = g[1] // 4, g[1] % 4
                    sp.dma_start(a3(slot, 2), wada_k[:, 2 * j:2 * j + 2, 2048 * part:2048 * (part + 1)]).then_inc(s, 16)
                elif k in ("ssm", "qi", "q", "gs", "ga"):
                    c0 = {"ssm": O_SSM, "qi": O_QI, "q": O_Q, "gs": O_GS, "ga": O_GA}[k] + 512 * g[1]
                    sp.dma_start(a3(slot, 8), win_k[:, :, c0:c0 + 512]).then_inc(s, 16)
                elif k == "misc":
                    v = a3(slot[:, 0:8 * 200], 8)
                    for c, c0, w in ((0, O_KI, 64), (64, O_K, 128), (192, O_WI, 8)):
                        sp.dma_start(v[:, :, c:c + w], win_k[:, :, c0:c0 + w]).then_inc(s, 16)
                elif k == "glu":
                    sp.dma_start(a3(slot[:, 0:2048], 4), rows(a["ssm_w_glu"][0])).then_inc(s, 16)
                elif k == "pp":
                    for j, w in enumerate(("w_proj_ssm", "w_proj_attn")):
                        sp.dma_start(a3(slot[:, 2048 * j:2048 * (j + 1)], 4),
                                     rows(a[w][0])[:, :, 512 * g[1]:512 * (g[1] + 1)]).then_inc(s, 16)
                elif k == "out":
                    sp.dma_start(a3(slot, 8), rows(a["w_out"][0])[:, :, 512 * g[1]:512 * (g[1] + 1)]).then_inc(s, 16)
                elif k == "sh":
                    for j, w in enumerate(("w_sh_gate", "w_sh_up")):
                        sp.dma_start(a3(slot, 8)[:, :, 256 * j:256 * (j + 1)], rows(a[w][0])).then_inc(s, 16)
                else:
                    sp.dma_start(a3(slot[:, 0:2048], 2), rows(a["w_sh_down"][0])).then_inc(s, 16)
                    sp.dma_start(a3(slot[:, 2048:2560], 8), rows(a["w_router"][0])).then_inc(s, 16)

            sp.dma_start(c_in, a["c"][0].rearrange("(p k) -> p k", k=KD)).then_inc(S["c_in"], 16)
            for n, c in enumerate((slice(0, 2 * DM), slice(2 * DM, 6 * DM))):
                if n == 1:
                    load(("A", 0))
                sp.wait_ge(S["ada_zero"], n + 1)
                sp.dma_start(ADA[0:1, c], a["b_ada"][0:1, c]).then_inc(b_in[n], 16)
            for g in list(ITEMS)[1:]:
                if g == ("misc", 0):
                    sp.wait_ge(S["zeros"], 1)
                    for j in range(TT):
                        for n in range(2):
                            sp.dma_start(ACC[n][P * j:P * (j + 1), :], W3).then_inc(S["acc_zero"], 16)
                if g == ("A", 5):
                    sp.wait_ge(S["u_rows"], 16 * TT)
                    for s in range(CH):
                        sp.dma_start(UB[0:NC, 512 * (7 - s):512 * (8 - s)],
                                     UD.rearrange("(c s) n -> c s n", s=CH)[:, s, :]).then_inc(S["u_chunks"], 16)
                load(g)
                if g == ("A", 1):
                    sp.dma_start(H[:], a["x"][0].rearrange("(t p) d -> p t d", p=P)).then_inc(S["x_in"], 16)

            def expert(r, blk):
                def src(w):
                    v = a[w][0].rearrange("(b r) k n -> b r k n", r=RING)
                    return v[bass.ds(blk, 1), r].rearrange("b k n -> (b k) n").rearrange("(p k) n -> p (k n)", p=P)
                sp.dma_start(wg[r], src("w_exp_gate")).then_inc(w_in_sem[r], 16)
                sp.dma_start(wu[r], src("w_exp_up")).then_inc(w_in_sem[r], 16)
                sp.dma_start(wdn[r], src("w_exp_down")).then_inc(w_in_sem[r], 16)

            sp.wait_ge(S["mixed"], KD)
            expert(0, 0)
            expert(1, 0)
            taken(sp, ("dn", TT - 1, 1))
            for n in range(2):
                sp.wait_ge(gathered[n], 16)
            expert(2, 0)
            expert(3, 0)
            with sp.Fori(1, NE // RING) as blk:
                for r in range(RING):
                    sp.wait_ge(S["expert_done"], blk * RING + (r - RING + 1))
                    expert(r, blk)

            def further(j, u):
                e = sp.value_load(ovrow[0:1, bass.ds(j + (MAXOV + 1), 1)], min_val=0, max_val=NE - 1)

                def src(w):
                    return a[w][0][bass.ds(e, 1)].rearrange("e k n -> (e k) n").rearrange("(p k) n -> p (k n)", p=P)
                sp.dma_start(wg[u], src("w_exp_gate")).then_inc(ov_w[u], 16)
                sp.dma_start(wu[u], src("w_exp_up")).then_inc(ov_w[u], 16)
                sp.dma_start(wdn[u], src("w_exp_down")).then_inc(ov_w[u], 16)

            sp.wait_ge(S["ov_row"], 16)
            n_ov = sp.value_load(ovrow[0:1, 0:1], min_val=0, max_val=MAXOV)
            for u in range(2):
                with sp.If(n_ov > u):
                    sp.wait_ge(S["expert_done"], NE - 3 + u)
                    further(u, u)
            with sp.Fori(0, 4) as ja:
                with sp.If(n_ov > ja * OVG):
                    with sp.Fori(0, OVG // 2) as jb:
                        jj = ja * (OVG // 2) + jb
                        for u in range(2):
                            j = jj * 2 + u
                            with sp.If(n_ov > j + 2):
                                sp.wait_ge(S["ov_y"], j + 3)
                                sp.wait_ge(S["ov_x"], j * 16 + 48)
                                further(j + 2, u)

            sp.wait_ge(S["all_added"], 1)
            for t in range(TT):
                sp.dma_start(XT[:, DM * t:DM * (t + 1)], ACC[0][P * t:P * (t + 1), :]).then_inc(sum_in[t], 16)
                sp.dma_start(ut4[:, t], ACC[1][P * t:P * (t + 1), :]).then_inc(sum_in[t], 16)
            for t in range(TT):
                sp.wait_ge(S["final"], t + 1)
                sp.dma_start(out[0, P * t:P * (t + 1), :], H[:, t, :]).then_inc(S["out_done"], 16)
            sp.wait_ge(S["out_done"], 16 * TT)

        @block.gpsimd
        def _(pool):
            n_o = [0]
            E = nc.gpsimd

            def link(ins):
                n_o[0] += 1
                ins.then_inc(S["pool_o"], 1)
                pool.wait_ge(S["pool_o"], n_o[0])

            link(E.memset(ones[:], 1.0))
            E.affine_select(out=sg, in_=ones[:, 0:1], compare_op=ALU.is_gt, fill=-1.0, base=64, pattern=[[0, 1]], channel_multiplier=-1)
            E.affine_select(out=nsg, in_=ones[:, 0:1], compare_op=ALU.is_ge, fill=-1.0, base=-64, pattern=[[0, 1]], channel_multiplier=1)
            E.memset(W3, 0.0).then_inc(S["zeros"], 1)
            E.iota(iota[:], [[1, SEQ]], base=0, channel_multiplier=0, allow_small_or_imprecise_dtypes=True)
            E.iota(tokp, [[0, TT]], base=0, channel_multiplier=1, allow_small_or_imprecise_dtypes=True)
            E.iota(tokt, [[1, TT]], base=-8, channel_multiplier=0, allow_small_or_imprecise_dtypes=True)
            E.iota(pp1, [[1, 1]], base=1, channel_multiplier=1, allow_small_or_imprecise_dtypes=True)
            link(E.memset(ident[:], 0.0))
            E.affine_select(out=lower[:], in_=ones[:], compare_op=ALU.is_gt, fill=0.0, base=0,
                            pattern=[[1, P]], channel_multiplier=-1)
            E.affine_select(out=ident[:], in_=ident[:], compare_op=ALU.not_equal, fill=1.0, base=0,
                            pattern=[[-1, P]], channel_multiplier=1).then_inc(S["consts"], 1)
            pool.wait_ge(S["consts"], 1)
            E.memset(GC, 0.0)
            E.memset(GS, 0.0).then_inc(S["scan_zero"], 1)
            lr, li = lam[:, 0:32], lam[:, 32:64]
            taken(pool, ("lam", 0))
            pool.wait_ge(S["dt_exp"], 1)

            def tt(o, x, y, op=ALU.mult):
                link(E.tensor_tensor(o, x, y, op))

            tt(m8, lr, dtb)
            tt(th, li, dtb)
            reduce_angle(E, link, th, N9[:, 0:32], T512[:, 0:32])
            tau = bc(iota[:, 0:9], G, 2)
            tt(a3(E9, 9), tau, bc(m8, 9, 1))
            tt(a3(A9, 9), tau, bc(th, 9, 1))
            reduce_angle(E, link, A9, N9, T512[:, 0:288])
            link(E.tensor_copy(th, A9[:, 256:288]))
            sin_cos_args(E, link, A9, N9, AimS, Are).then_inc(S["angles"], 1)
            pool.wait_ge(S["sines"], 1)
            tt(Are, Are, E9)
            tt(AimS, AimS, E9)
            link(E.tensor_copy(m8, E9[:, 256:288]))
            nr, den, fr, fi, t1 = fcol
            are1, aim1 = Are[:, 32:64], AimS[:, 32:64]
            link(E.tensor_scalar(nr, are1, -1.0, None, ALU.add))
            tt(den, lr, lr)
            tt(t1, li, li)
            tt(den, den, t1, ALU.add)
            tt(fr, nr, lr)
            tt(t1, aim1, li)
            tt(fr, fr, t1, ALU.add)
            tt(fi, aim1, lr)
            tt(t1, nr, li)
            tt(fi, fi, t1, ALU.subtract)
            link(E.memset(D0[:, 0:32], -1.0))
            tt(den, den, D0[:, 0:32], ALU.pow)
            tt(fr, fr, den)
            tt(fi, fi, den)
            link(E.tensor_scalar(fi, fi, nsg, None, ALU.mult))
            link(E.tensor_scalar(AimS, AimS, nsg, None, ALU.mult))
            pool.wait_ge(S["bt_in"], 64)
            frb, fib = bc(fr, GH, 2), bc(fi, GH, 2)
            tt(a3(Xb, G), a3(B1, G), frb)
            tt(a3(T512, G), a3(B2, G), fib)
            tt(Xb, Xb, T512, ALU.add)
            tt(a3(Zb, G), a3(B2, G), frb)
            tt(a3(T512, G), a3(B1, G), fib)
            E.tensor_tensor(Zb, Zb, T512, ALU.subtract).then_inc(S["b_ok"], 1)
            pool.wait_ge(S["b_ok"], 1)

            def powers(tab, lo, n, q):
                v = a3(tab, 9)[:, lo:lo + n, QG * q:QG * (q + 1)].rearrange("p t g -> p g t")
                return bc(v, GH, 3)

            def coef(tab, n, q):
                return bc(a3(tab, G)[:, QG * q:QG * (q + 1), :], n, 2)

            def v4(ap):
                return ap.rearrange("p (g t h) -> p g t h", g=QG, h=GH)

            def causal(i):
                pool.wait_ge(S["relu_free"], NH * i)
                d = sc_of[i][:, P * i:P * (i + 1)]
                E.affine_select(out=d, in_=d, compare_op=ALU.is_ge, fill=MASKED, base=0,
                                pattern=[[-1, P]], channel_multiplier=1).then_inc(S["causal"], 1)

            def s5_tables(q):
                CA = CAb[q % 2]
                if q:
                    taken(pool, ("bT", q - 1, 1))
                if q > 1:
                    taken(pool, ("y", q - 2, 1))
                if q == 1:
                    taken(pool, ("cT", 3))
                tt(v4(BA), coef(Xb, 8, q), powers(Are, 0, 8, q))
                tt(v4(CA[:, 0:1024]), coef(Zb, 8, q), powers(AimS, 0, 8, q))
                E.tensor_tensor(BA, BA, CA[:, 0:1024], ALU.add).then_inc(S["ba_ok"], 1)
                pool.wait_ge(S["ba_ok"], q + 1)
                taken(pool, ("cT", 3))
                tt(v4(CA), coef(X, 9, q), powers(Are, 0, 9, q))
                for lo, n in ((0, 4), (4, 4), (8, 1)):
                    tt(v4(T512[:, 0:QG * n * GH]), coef(Z, n, q), powers(AimS, lo, n, q))
                    last = E.tensor_tensor(v4(CA)[:, :, lo:lo + n], v4(CA)[:, :, lo:lo + n],
                                           v4(T512[:, 0:QG * n * GH]), ALU.subtract)
                    if lo < 8:
                        link(last)
                last.then_inc(S["ca_ok"], 1)
                pool.wait_ge(S["ca_ok"], q + 1)
                if q:
                    taken(pool, ("y", q - 1, 1))
                tt(v4(W2), coef(Z, 8, q), powers(Are, 1, 8, q))
                for lo in (0, 4):
                    tt(v4(T512), coef(X, 4, q), powers(AimS, lo + 1, 4, q))
                    last = E.tensor_tensor(v4(W2)[:, :, lo:lo + 4], v4(W2)[:, :, lo:lo + 4], v4(T512), ALU.add)
                    if lo == 0:
                        link(last)
                last.then_inc(S["w2_ok"], 1)
                pool.wait_ge(S["w2_ok"], q + 1)

            s5_tables(0)
            s5_tables(1)
            causal(1)
            causal(2)
            s5_tables(2)
            causal(3)
            s5_tables(3)

            taken(pool, ("y", NQ - 1, 1))
            for i in range(TT):
                last = E.iota(Mb[i], [[1, P * (i + 1)]], base=-P * i, channel_multiplier=-1,
                              allow_small_or_imprecise_dtypes=True)
                if i == 0:
                    link(last)
                    last = E.affine_select(out=Mb[0], in_=Mb[0], compare_op=ALU.is_ge, fill=MASKED, base=0,
                                           pattern=[[-1, P]], channel_multiplier=1)
                last.then_inc(S["dist"], 1)

            for t in range(TT):
                pool.wait_ge(S["u2_tile"], t + 1)
                pool.dma_start(U2D[P * t:P * (t + 1), :], u2t4[:, t, :]).then_inc(S["u2_rows"], 16)
            pool.wait_ge(S["u2_rows"], 16 * TT)
            taken(pool, ("u2T", TT - 1, 1))
            pool.dma_start(rbias, a["router_bias"][0:1, :].broadcast_to((P, NE))).then_inc(S["bias_in"], 16)
            E.iota(ovc, [[1, NE], [0, XB]], base=0, channel_multiplier=0, allow_small_or_imprecise_dtypes=True)
            E.iota(ovt, [[0, NE], [P, XB]], base=P, channel_multiplier=0, allow_small_or_imprecise_dtypes=True)
            E.memset(UB[:, 0:816], 0.0)
            E.memset(UB[:, 816:816 + TT * NEP], -1.0)
            link(E.memset(scr[:, 1952:2016], 1.0))
            E.affine_select(out=lt8, in_=lt8, compare_op=ALU.is_gt, fill=0.0, base=0,
                            pattern=[[1, 8], [-1, 8]], channel_multiplier=0).then_inc(S["masks"], 1)

            E.memset(XT[:, 0:2048], 0.0).then_inc(S["x_zero"], 1)
            pool.wait_ge(S["x_zero"], 1)

            def gather(par, col, s):
                pool.sem_inc(S["pool_turn"], 1)
                E.indirect_dma_start(xg[par], None, U2D, bass.IndirectOffsetOnAxis(idx[:, col:col + 1], 0),
                                     bounds_check=SEQ - 1, oob_is_err=False).then_inc(s, 16)

            def add(par, s):
                pool.sem_inc(S["pool_turn"], 1)
                E.indirect_dma_start(ACC[par], bass.IndirectOffsetOnAxis(adx[:, par:par + 1], 0), ye[par], None,
                                     compute_op=ALU.add, bounds_check=SEQ - 1, oob_is_err=False).then_inc(s, 16)

            pool.wait_ge(S["acc_zero"], 32 * TT)

            def add_expert(blk, r):
                e = blk * RING + r
                pool.wait_ge(S["y_out_s"], e + 1)
                pool.wait_ge(S["y_out_v"], e + 1)
                added(pool, blk, r - 2)
                add(r % 2, y_added[r % 2])

            for _ in range(2):
                pool.sem_inc(S["ov_y"], 1)
                pool.sem_inc(S["ov_yo"], 1)
            for e in range(2):
                pool.wait_ge(S["list_out"], e + 1)
                gather(e, e, gathered[e])

            pool.wait_ge(S["ov_list"], 1)
            pool.dma_start(OVD, ovi[0:MAXOV + 1, :]).then_inc(S["ov_out"], 16)
            pool.wait_ge(S["ov_out"], 16)
            with nc.allow_non_contiguous_dma(reason="96 values"):
                pool.dma_start(ovrow[:, 0:3 * (MAXOV + 1)].rearrange("a (c j) -> a c j", c=3),
                               OVD.rearrange("(a j) c -> a c j", a=1)).then_inc(S["ov_row"], 16)

            def step(blk, r):
                e = blk * RING + r
                if follows(blk, r, 2):
                    pool.wait_ge(S["list_out"], e + 3)
                    pool.wait_ge(S["x_tr"], e + 1)
                    gather(r % 2, (r + 2) % RING, gathered[r % 2])
                if not is_first(blk, r):
                    add_expert(blk, r - 1)

            over_blocks(step, pool)
            pool.wait_ge(S["ov_idx"], 1)
            gather(0, 0, S["ov_x"])
            add_expert(NE // RING - 1, RING - 1)
            added(pool, NE // RING - 1, RING - 2)
            added(pool, NE // RING - 1, RING - 1)
            for _ in range(2):
                pool.sem_inc(S["ov_go"], 1)

            pool.wait_ge(S["ov_row"], 16)
            n_ov = pool.value_load(ovrow[0:1, 0:1], min_val=0, max_val=MAXOV)
            with pool.Fori(0, 4) as ja:
                with pool.If(n_ov > ja * OVG):
                    with pool.Fori(0, OVG // 2) as jb:
                        jj = ja * (OVG // 2) + jb
                        for u in range(2):
                            j = jj * 2 + u
                            with pool.If(n_ov > j):
                                pool.wait_ge(S["ov_idx"], j + 2)
                                gather(1 - u, 1 - u, S["ov_x"])
                                pool.wait_ge(S["ov_yo"], j * 2 + 4)
                                add(u, S["ov_add"])
                                pool.wait_ge(S["ov_add"], j * 16 + 16)
                                pool.sem_inc(S["ov_go"], 1)
            pool.wait_ge(S["ov_x"], n_ov * 16 + 16)
            pool.sem_inc(S["all_added"], 1)
            for t in range(TT):
                pool.wait_ge(sum_in[t], 32)
                E.tensor_tensor(ut4[:, t], ut4[:, t], XT[:, DM * t:DM * (t + 1)], ALU.add).then_inc(S["sums_joined"], 1)

        @block.scalar
        def _(act):
            A = nc.scalar.activation
            n_o = [0]

            def link(ins):
                n_o[0] += 1
                ins.then_inc(S["scalar_o"], 1)
                act.wait_ge(S["scalar_o"], n_o[0])

            for j, w in enumerate(("ssm_lambda_re", "ssm_lambda_im")):
                for half in range(2):
                    act.dma_start(lamn[:, P * j + 64 * half:P * j + 64 * half + 64], a[w][0]).then_inc(S["lam_in"], 16)
            act.dma_start(dtb, a["ssm_log_dt"][0:1, :].broadcast_to((P, G))).then_inc(S["dt_in"], 16)
            with nc.allow_non_contiguous_dma(reason="1024 values"):
                act.dma_start(g1T, a["norm1_g"][0].rearrange("(k p) -> p k", p=P)).then_inc(S["g1_in"], 16)
            act.wait_ge(S["c_in"], 16)
            A(csil, c_in, ACT.Silu).then_inc(S["c_silu"], 1)
            act.wait_ge(S["dt_in"], 16)
            A(dtb, dtb, ACT.Exp).then_inc(S["dt_exp"], 1)
            for j in range(4):
                for n, pair in enumerate((("ssm_c_re", "ssm_c_im"), ("ssm_c_im", "ssm_c_re"))):
                    for half, w in enumerate(pair):
                        act.dma_start(cn[:, 2 * j + n, 64 * half:64 * half + 64],
                                       a[w][0, 8 * j:8 * j + 8].rearrange("g h p -> (g h) p")).then_inc(S["ct_in"], 16)
            for dst, pair in ((B1, ("ssm_b_re", "ssm_b_im")), (B2, ("ssm_b_im", "ssm_b_re"))):
                for half, w in enumerate(pair):
                    act.dma_start(a3(dst, G)[64 * half:64 * half + 64], a[w][0].rearrange("g p h -> p g h")).then_inc(S["bt_in"], 16)
            with nc.allow_non_contiguous_dma(reason="1024 values in all"):
                act.dma_start(dsk, a["ssm_d"][0].rearrange("(g h) -> h g", h=GH)).then_inc(S["dsk_in"], 16)
                act.dma_start(bglu, a["ssm_b_glu"][0].rearrange("(m p) -> p m", p=P)).then_inc(S["bglu_in"], 16)

            takes(A(lam, done(act, ("lam", 0))[:, 0:64], ACT.Copy), ("lam", 0))
            act.wait_ge(S["x_in"], 16)
            for t in range(TT):
                link(A(UB[:, DM:2 * DM], H[:, t, :], ACT.Square, accum_out=ssq[:, t:t + 1]))
            A(junk1, ssq[:, 3:4], ACT.Copy).then_inc(S["squares"], 1)

            def root(c, count):
                act.wait_ge(S["inverse"], count)
                A(rstd[:, c], rstd[:, c], ACT.Sqrt).then_inc(S["root"], 1)

            def out_copy(g, dst, width=512, func=ACT.Copy, view=None):
                b = done(act, g)
                src = b[:, 0:width] if view is None else view(b)
                takes(A(dst, src, func), g)

            root(slice(0, TT), 1)
            act.wait_ge(S["rstd_ok"], 1)
            for t in range(TT):
                A(ut4[:, t], H[:, t], ACT.Copy, scale=rstd[:, t:t + 1]).then_inc(S["u_tile"], 1)
            for t in range(TT):
                for n in range(2):
                    out_copy(("uT", t, n), uT[:, 4 * n:4 * n + 4, P * t:P * (t + 1)], view=lambda b: a3(b[:, :], 4))
            act.wait_ge(S["angles"], 1)
            A(E9, E9, ACT.Exp)
            A(AimS, AimS, ACT.Sin)
            A(Are, Are, ACT.Sin).then_inc(S["sines"], 1)

            def s5_build(q):
                for n in range(2):
                    out_copy(("bT", q, n), W1[:, 512 * n:512 * (n + 1)])

            def phases(q):
                act.wait_ge(S["phase_args"], q + 1)
                A(SIN, SIN, ACT.Sin)
                A(COS, COS, ACT.Sin).then_inc(S["phases"], 1)

            def arrange_u(q):
                if q == 0:
                    act.wait_ge(S["u_chunks"], 16 * CH)
                c0 = GH * QG * q
                src = UB[0:NC, :].rearrange("c (s n) -> c s n", s=CH)[:, :, c0:c0 + GH * QG]
                A(uperm.rearrange("c (g s h) -> c s g h", g=QG, s=CH), src.rearrange("c s (g h) -> c s g h", g=QG),
                  ACT.Copy).then_inc(S["u_perm"], 1)

            def s5_apply(q):
                out_copy(("uc", q), uc)
                if q + 1 < NQ:
                    arrange_u(q + 1)
                taken(act, ("K", q, 1))
                if q == 0:
                    act.wait_ge(S["acc_zero"], 32 * TT)
                for j in range(CH):
                    s = CH - 1 - j
                    act.dma_start(a3(W3, QG)[GH * j:GH * (j + 1), :, GH * s:P],
                                  a3(K16, QG)[:, :, 0:GH * (CH - s)]).then_inc(S["toeplitz"], 16)
                out_copy(("gs", q), sgb[:, q, :])
                Yv = UB[0:NC, :].rearrange("c (t g h) -> c g t h", t=CH, h=GH)
                for n in range(2):
                    g0 = QG * q + 4 * n
                    for g in range(4):
                        b = done(act, ("y", q, n))
                        ins = A(Yv[:, g0 + g], b[0:NC, P * g:P * (g + 1)].rearrange("c (t h) -> c t h", h=GH), ACT.Copy)
                    takes(ins, ("y", q, n))

            def indexer(i):
                w = P * (i + 1)
                for h in range(NH):
                    n = NH * (i - 1) + h
                    if n >= 2:
                        act.wait_ge(S["relu_free"], n - 1)
                    out_copy(("idx", i, h), relu[:, n % 2, 0:w], w, ACT.Relu)

            act.wait_ge(S["modulation"], 1)
            taken(act, ("uT", TT - 1, 1))
            for k in range(1, KD, 2):
                A(uT[:, k], uT[:, k], ACT.Identity, scale=scT[:, k:k + 1], bias=shT[:, k:k + 1]).then_inc(S["u_ok_s"], 1)
            for t in range(TT):
                out_copy(("ssm", t), unat[:, t, :])
                taken(act, ("ssm", t))
                act.dma_start(UD[P * t:P * (t + 1), :], unat[:, t, :]).then_inc(S["u_rows"], 16)
            b = done(act, ("kkT", 0))
            for half in range(2):
                A(kiT[64 * half:64 * half + 64], b[0:64, :], ACT.Copy)
                ins = A(kT[64 * half:64 * half + 64], b[64:128, :], ACT.Copy)
            takes(ins, ("kkT", 0))
            b = done(act, ("vwT", 0))
            takes(A(vwT, b[0:72, :], ACT.Copy), ("vwT", 0))
            out_copy(("vw", 0), vw[:], view=lambda b: a3(b[:, 0:288], 4))
            act.wait_ge(S["u_rows"], 16 * TT)
            for m in range(4):
                out_copy(("qiT", m), qiT[:, m, :])
            phases(0)
            indexer(1)
            arrange_u(0)
            s5_build(0)
            indexer(2)
            s5_apply(0)
            phases(1)
            s5_build(1)
            indexer(3)
            s5_apply(1)
            phases(2)
            s5_build(2)
            s5_apply(2)
            phases(3)
            s5_build(3)
            s5_apply(3)
            for m in range(4):
                out_copy(("qT", m), qT[:, m, :])
            A(sgb, sgb, ACT.Sigmoid)
            for m in range(4):
                out_copy(("yT", m), yT[:, m, :], func=ACT.Gelu_apprx_tanh)

            for i in range(TT):
                w = P * (i + 1)

                def prob(h):
                    n = NH * i + h
                    act.wait_ge(S["t_max"], n + 1)
                    A(tb[n % 3][:, 0:w], tb[n % 3][:, 0:w], ACT.Exp, bias=nb[:, n:n + 1], scale=2.0 ** -(h + 1),
                      accum_out=rsum[:, n:n + 1]).then_inc(S["prob"], 1)

                prob(0)
                for h in range(NH):
                    if h + 1 < NH:
                        prob(h + 1)
                    n = NH * i + h
                    if n >= 2:
                        act.wait_ge(S["av_done"], n - 1)
                    out_copy(("pT", i, h), pTb[n % 2][:, 0:w], w)
                    if (i, h) in FILL:
                        name, d = FILL[i, h]
                        out_copy((name, d), sab[:, d, :] if name == "ga" else sgb2[:, d - 4, :])
                    if i and h == 1:
                        out_copy(("yaT", i - 1), yaT[:, :, P * (i - 1):P * i], view=lambda b: a3(b[:, :], 4))
            act.wait_ge(S["bglu_in"], 16)
            taken(act, ("ga", 3))
            taken(act, ("gs", 7))
            A(sab, sab, ACT.Sigmoid)
            A(sgb2, sgb2, ACT.Sigmoid).then_inc(S["gates_ok"], 1)
            for m in range(4):
                b = done(act, ("glu", m))
                if m >= 2:
                    act.wait_ge(S["y2_ok"], m - 1)
                takes(A(tb[m % 2], b[:], ACT.Sigmoid, bias=bglu[:, m:m + 1]), ("glu", m))
            out_copy(("yaT", TT - 1), yaT[:, :, P * (TT - 1):], view=lambda b: a3(b[:, :], 4))
            act.wait_ge(S["mixed"], 4)
            for d in range(4, 8):
                out_copy(("ga", d), sab[:, d - 4, :], func=ACT.Sigmoid)
            act.wait_ge(S["relu_free"], 3 * NH)
            act.dma_start(GB[:], a["norm2_g"][0:1, :].broadcast_to((P, DM))).then_inc(S["norm_in"], 16)
            for t in range(TT + 2):
                if t < TT:
                    act.wait_ge(S["h_out"], 2 * t + 2)
                    A(ADA[:, DM:2 * DM], H[:, t, :], ACT.Square, accum_out=ssq[:, t:t + 1]).then_inc(S["squares"], 1)
                    root(slice(t, t + 1), 2 + t)
                if t >= 2:
                    for n in range(2):
                        out_copy(("u2T", t - 2, n), uT[:, 4 * n:4 * n + 4, P * (t - 2):P * (t - 1)], view=lambda b: a3(b[:, :], 4))
            b = done(act, ("rt", 0))
            takes(A(scT64, b[0:NE, :], ACT.Sigmoid), ("rt", 0))
            out_copy(("rtT", 0), sct, view=lambda b: a3(b[:, 0:256], 4))
            act.wait_ge(S["u2_rows"], 16 * TT)
            for m in range(2):
                out_copy(("sh", m), XT[:, 2048 + 512 * m:2560 + 512 * m], func=ACT.Silu)
            act.wait_ge(S["u2_tile"], TT)
            act.dma_start(GB[:], a["norm_f_g"].rearrange("(a d) -> a d", a=1).broadcast_to((P, DM))).then_inc(S["norm_in"], 16)

            def copy_x(par, tr, count, s):
                act.wait_ge(tr, count)
                A(xgT[par][:, 0:4], a3(ps[1][:, :], 4), ACT.Copy).then_inc(s, 1)

            def silu(gu, count, s):
                act.wait_ge(gu, count)
                A(hg, ps[0][:, 0:ED], ACT.Silu).then_inc(s, 1)

            def result(blk, r):
                e = blk * RING + r
                act.wait_ge(S["expert_done"], e + 1)
                added(act, blk, r - 2)
                A(ye[r % 2][:, 512:1024], ps[7][:, :], ACT.Copy, scale=gat[:, r % RING:r % RING + 1]).then_inc(S["y_out_s"], 1)

            def step(blk, r):
                e = blk * RING + r
                silu(S["gu_done"], e + 1, S["g_silu"])
                if follows(blk, r, 1):
                    copy_x((r + 1) % 2, S["x_tr"], e + 2, S["x_out_s"])
                if not is_first(blk, r):
                    result(blk, r - 1)

            taken(act, ("dn", TT - 1, 1))
            copy_x(0, S["x_tr"], 1, S["x_out_s"])
            over_blocks(step, act)
            result(NE // RING - 1, RING - 1)

            copy_x(0, S["ov_xt"], 1, S["ov_xs"])
            act.wait_ge(S["ov_row"], 16)
            n_ov = act.value_load(ovrow[0:1, 0:1], min_val=0, max_val=MAXOV)
            with act.Fori(0, 4) as ja:
                with act.If(n_ov > ja * OVG):
                    with act.Fori(0, OVG // 2) as jb:
                        jj = ja * (OVG // 2) + jb
                        for u in range(2):
                            j = jj * 2 + u
                            with act.If(n_ov > j):
                                silu(S["ov_gu"], j + 1, S["ov_silu"])
                                copy_x(1 - u, S["ov_xt"], j + 2, S["ov_xs"])
                                act.wait_ge(S["ov_y"], j + 3)
                                act.wait_ge(S["ov_go"], j + 1)
                                A(ye[u][:, 512:1024], ps[7][:, :], ACT.Copy, scale=gat[:, u:u + 1]).then_inc(S["ov_yo"], 1)
            for t in range(TT):
                act.wait_ge(S["fin_add"], t + 1)
                A(XT[:, DM * t:DM * (t + 1)], H[:, t, :], ACT.Square, accum_out=ssq[:, t:t + 1]).then_inc(S["fin_sq"], 1)
                root(slice(t, t + 1), 6 + t)

        @block.vector
        def _(dve):
            V = nc.vector
            n_o = [0]

            def link(ins):
                n_o[0] += 1
                ins.then_inc(S["vector_o"], 1)
                dve.wait_ge(S["vector_o"], n_o[0])

            def signal(ins, s, count):
                ins.then_inc(S[s], 1)
                dve.wait_ge(S[s], count)

            def out(ins, g):
                takes(ins, g)
                taken(dve, g)

            V.memset(ADA[:, 0:2 * DM], 0.0).then_inc(S["ada_zero"], 1)
            V.memset(ADA[:, 2 * DM:6 * DM], 0.0).then_inc(S["ada_zero"], 1)
            dve.wait_ge(b_in[0], 16)
            dve.wait_ge(S["c_silu"], 1)

            def ada_half(n, k):
                part, j = n // 4, n % 4
                acc = ADA[:, 2048 * part:2048 * (part + 1)]
                return V.scalar_tensor_tensor(acc, a3(arrived(dve, ("A", n)), 2)[:, k], csil[:, 2 * j + k:2 * j + k + 1], acc,
                                              ALU.mult, ALU.add)

            def ada_piece(n):
                link(ada_half(n, 0))
                signal(ada_half(n, 1), "ada_sum", n + 1)

            def ada_out(n):
                out(V.tensor_copy(ADA[:, 512 * n:512 * (n + 1)], done(dve, ("ada", n))[:]), ("ada", n))

            def rms_scale(c, count):
                link(V.tensor_scalar(var[:, c], ssq[:, c], 1.0 / DM, EPS, ALU.mult, ALU.add))
                V.reciprocal(rstd[:, c], var[:, c]).then_inc(S["inverse"], 1)
                dve.wait_ge(S["root"], count)
                link(V.tensor_tensor(newt[:, c], rstd[:, c], rstd[:, c], ALU.mult))
                link(V.tensor_tensor(newt[:, c], newt[:, c], var[:, c], ALU.mult))
                link(V.tensor_scalar(newt[:, c], newt[:, c], -0.5, 1.5, ALU.mult, ALU.add))
                link(V.tensor_tensor(rstd[:, c], rstd[:, c], newt[:, c], ALU.mult))

            for n in range(3):
                ada_piece(n)
            dve.wait_ge(S["squares"], 1)
            rms_scale(slice(0, TT), 1)
            V.tensor_copy(junk1, rstd[:, 0:1]).then_inc(S["rstd_ok"], 1)
            ada_piece(3)
            dve.wait_ge(S["g1_in"], 16)
            b = done(dve, ("mod", 0))
            V.tensor_copy(shT, b[:, 0:KD])
            out(V.scalar_tensor_tensor(scT, b[:, KD:2 * KD], 1.0, g1T, ALU.add, ALU.mult), ("mod", 0))
            V.tensor_copy(junk1, scT[:, 0:1]).then_inc(S["modulation"], 1)
            taken(dve, ("uT", TT - 1, 1))
            for k in range(0, KD, 2):
                V.tensor_scalar(uT[:, k], uT[:, k], scT[:, k:k + 1], shT[:, k:k + 1], ALU.mult, ALU.add).then_inc(S["u_ok_v"], 1)

            def s5_kernel(q):
                if q:
                    dve.wait_ge(S["toeplitz"], 16 * CH * q)
                dve.wait_ge(S["dsk_in"], 16)
                link(V.tensor_tensor(a3(kd, QG), bc(ident[0:GH, 0:GH], QG, 1), bc(dsk[:, QG * q:QG * (q + 1)], GH, 2), ALU.mult))
                for n in range(2):
                    b = a3(done(dve, ("K", q, n))[0:GH, :], 4)
                    k = a3(K16[:, 512 * n:512 * (n + 1)], 4)
                    V.tensor_copy(k[:, :, GH:P], b[:, :, GH:P])
                    out(V.tensor_tensor(k[:, :, 0:GH], b[:, :, 0:GH], a3(kd, QG)[:, 4 * n:4 * n + 4], ALU.add), ("K", q, n))

            def s5_scan(q):
                dve.wait_ge(S["phases"], q + 1)
                V.tensor_scalar(SIN, SIN, sg, None, ALU.mult)
                link(V.tensor_copy(a3(D0, QG), bc(m8[:, QG * q:QG * (q + 1)], NC, 2)))
                link(V.memset(a3(D0, QG)[:, :, 0:1], 0.0))
                b = done(dve, ("v1", q))
                takes(V.tensor_tensor(Vt, b[:], COS, ALU.mult), ("v1", q))
                b = done(dve, ("v2", q))
                takes(V.tensor_tensor(GV, b[:], SIN, ALU.mult), ("v2", q))
                taken(dve, ("v2", q))
                link(V.tensor_tensor(Vt, Vt, GV, ALU.add))
                link(V.tensor_tensor_scan(GV, D0, Vt, 0.0, ALU.mult, ALU.add))
                g3 = a3(GV, QG)[:, :, 0:NC - 1]
                V.tensor_tensor(a3(GC, QG)[:, :, 1:NC], g3, a3(COS, QG)[:, :, 0:NC - 1], ALU.mult)
                V.tensor_tensor(a3(GS, QG)[:, :, 1:NC], g3, a3(SIN, QG)[:, :, 0:NC - 1], ALU.mult).then_inc(S["rotated"], 1)

            def s5_phases(q):
                dve.wait_ge(S["b_ok"], 1)
                link(V.tensor_tensor(a3(D0, QG), bc(iota[:, 0:NC], QG, 1), bc(th[:, QG * q:QG * (q + 1)], NC, 2), ALU.mult))
                reduce_angle(V, link, D0, SIN, COS)
                signal(sin_cos_args(V, link, D0, GV, SIN, COS), "phase_args", q + 1)

            def index_scores(i):
                w = P * (i + 1)
                for h in range(NH):
                    n = NH * (i - 1) + h
                    taken(dve, ("idx", i, h))
                    wcol = wis[:, i, h:h + 1]
                    if h == 0:
                        ins = V.tensor_scalar(sc_of[i], relu[:, n % 2, 0:w], wcol, None, ALU.mult)
                    else:
                        ins = V.scalar_tensor_tensor(sc_of[i], relu[:, n % 2, 0:w], wcol, sc_of[i], ALU.mult, ALU.add)
                    signal(ins, "relu_free", n + 1)

            def top_k(i, r0, r1):
                if r0 == 0:
                    dve.wait_ge(S["causal"], i)
                for _ in range(r0, r1):
                    link(V.max(top8, sc_of[i]))
                    link(V.match_replace(sc_of[i], top8, sc_of[i], TAKEN))

            dve.wait_ge(S["consts"], 1)
            for j in range(4):
                b = done(dve, ("cT", j))
                V.tensor_scalar(X[:, P * j:P * (j + 1)], b[:, 0:P], sg, None, ALU.mult)
                takes(V.tensor_scalar(Z[:, P * j:P * (j + 1)], b[:, P:2 * P], nsg, None, ALU.mult), ("cT", j))

            dve.wait_ge(b_in[1], 16)
            dve.wait_ge(S["scan_zero"], 1)
            ada_piece(4)
            taken(dve, ("vw", 0))
            link(V.tensor_scalar(wis, vw[:, :, HD:HD + NH], float(NH * 64) ** -0.5, None, ALU.mult))
            s5_phases(0)
            ada_piece(5)
            index_scores(1)
            s5_kernel(0)
            index_scores(2)
            s5_scan(0)
            s5_phases(1)
            s5_kernel(1)
            index_scores(3)
            s5_scan(1)
            s5_phases(2)
            s5_kernel(2)
            ada_piece(6)
            s5_scan(2)
            s5_phases(3)
            top_k(1, 0, 4)
            s5_kernel(3)
            top_k(1, 4, 10)
            s5_scan(3)
            top_k(1, 10, 16)
            ada_piece(7)
            top_k(2, 0, 16)

            def attended(i):
                hd = slice(NH * i, NH * (i + 1))
                dve.wait_ge(S["prob"], NH * (i + 1))
                link(V.reciprocal(rinv[:, hd], rsum[:, hd]))
                dve.wait_ge(S["av_done"], NH * (i + 1))
                if i:
                    done(dve, ("yaT", i - 1))
                V.tensor_tensor(a3(yat, NH), a3(ps[6 + i % 2][:, :], NH), bc(rinv[:, hd], HD, 2), ALU.mult).then_inc(S["y_att"], 1)

            for i in range(TT):
                w = P * (i + 1)
                dve.wait_ge(S["dist"], i + 1)
                if i:
                    link(V.tensor_scalar(sc_of[i], sc_of[i], LIM, MASKED, ALU.is_gt, ALU.mult))
                    link(V.tensor_tensor(Mb[i], Mb[i], sc_of[i], ALU.add))
                for h in range(NH):
                    n = NH * i + h
                    if n < TOPK // 8:
                        top_k(3, n, n + 1)
                    if n >= 3:
                        done(dve, ("pT", (n - 3) // NH, (n - 3) % NH))
                    b = done(dve, ("lg", i, h))
                    t = tb[n % 3][:, 0:w]
                    out(V.scalar_tensor_tensor(t, b[:, 0:w], 2.0 ** (h + 1) * HD ** -0.5, Mb[i], ALU.mult, ALU.add), ("lg", i, h))
                    link(V.reduce_max(mx[:, n:n + 1], t, axis=AX.X))
                    V.tensor_scalar(nb[:, n:n + 1], mx[:, n:n + 1], -(2.0 ** -(h + 1)), None, ALU.mult).then_inc(S["t_max"], 1)
                    if i and h == 1:
                        attended(i - 1)
                    if (i, h - 2) in FILL:
                        k = list(FILL).index((i, h - 2))
                        if k % 2 == 0:
                            link(ada_half(8 + k // 2, 0))
                        else:
                            signal(ada_half(8 + k // 2, 1), "ada_sum", 9 + k // 2)
            attended(TT - 1)

            for m in range(4):
                taken(dve, ("glu", m))
                done(dve, ("glu", 3))
                V.tensor_tensor(y2T[:, m, :].rearrange("p (c t) -> p t c", t=CH), a3(yT[:, m, :], CH), a3(tb[m % 2], CH),
                                ALU.mult).then_inc(S["y2_ok"], 1)
            for n in range(4, 12):
                ada_out(n)
            dve.wait_ge(S["gates_ok"], 1)
            for d in range(KD):
                taken(dve, ("ga", d))
                b = done(dve, ("ps", d))
                takes(V.tensor_tensor(mixT[:, d], b[:], (sgb, sgb2)[d // 4][:, d % 4], ALU.mult), ("ps", d))
                b = done(dve, ("pa", d))
                out(V.tensor_tensor(tmpv, b[:], sab[:, d % 4], ALU.mult), ("pa", d))
                signal(V.tensor_tensor(mixT[:, d], mixT[:, d], tmpv, ALU.add), "mixed", d + 1)
            dve.wait_ge(S["norm_in"], 16)
            link(V.scalar_tensor_tensor(ADA[:, 4 * DM:5 * DM], ADA[:, 4 * DM:5 * DM], 1.0, GB[:], ALU.add, ALU.mult))
            for t in range(TT):
                for n in range(2):
                    b = done(dve, ("out", t, n))
                    hh = H[:, t, 512 * n:512 * (n + 1)]
                    out(V.tensor_tensor(tmp2, b[:], ADA[:, 2 * DM + 512 * n:2 * DM + 512 * (n + 1)], ALU.mult), ("out", t, n))
                    signal(V.tensor_tensor(hh, hh, tmp2, ALU.add), "h_out", 2 * t + n + 1)
                dve.wait_ge(S["squares"], 2 + t)
                rms_scale(slice(t, t + 1), 2 + t)
                link(V.scalar_tensor_tensor(u2t4[:, t], H[:, t], rstd[:, t:t + 1], ADA[:, 4 * DM:5 * DM], ALU.mult, ALU.mult))
                signal(V.tensor_tensor(u2t4[:, t], u2t4[:, t], ADA[:, 3 * DM:4 * DM], ALU.add), "u2_tile", t + 1)

            dve.wait_ge(S["bias_in"], 16)
            dve.wait_ge(S["masks"], 1)
            taken(dve, ("rtT", 0))
            link(V.tensor_tensor(bia, sct, bc(rbias, TT, 1), ALU.add))
            b4 = bia.rearrange("p t (g k) -> p t g k", g=NGR)
            for t in range(TT):
                for g in range(NGR):
                    ins = V.max(m2[:, t, g], b4[:, t, g])
            link(ins)
            link(V.tensor_tensor(gsum, m2[:, :, :, 0], m2[:, :, :, 1], ALU.add))
            mine, other = bc(gsum, NGR, 3), bc(gsum, NGR, 2)
            link(V.tensor_tensor(cmp, other, mine, ALU.is_gt))
            link(V.tensor_tensor(cmp2, other, mine, ALU.is_equal))
            link(V.tensor_tensor(cmp2, cmp2, bc(lt8, TT, 1), ALU.mult))
            link(V.tensor_tensor(cmp, cmp, cmp2, ALU.add))
            link(V.tensor_reduce(rank, cmp, axis=AX.X, op=ALU.add))
            link(V.tensor_scalar(gm, rank, float(TG) - 0.5, MASKED, ALU.is_gt, ALU.mult))
            link(V.tensor_tensor(wk.rearrange("p t (g k) -> p t g k", g=NGR), b4, bc(gm, EPG, 3), ALU.add))
            for t in range(TT):
                link(V.max(m2[:, t, 0], wk[:, t]))
                link(V.match_replace(wk[:, t], m2[:, t, 0], wk[:, t], TAKEN))
            signal(V.tensor_scalar(Mm, wk, LIM, None, ALU.is_lt), "slots", 1)
            link(V.tensor_tensor(bia, sct, Mm, ALU.mult))
            link(V.tensor_reduce(gsm, bia, axis=AX.X, op=ALU.add))
            link(V.reciprocal(gsm, gsm))
            link(V.tensor_scalar(gsm, gsm, ROUTED_SCALE, None, ALU.mult))
            link(V.tensor_tensor(r1, bia, bc(gsm, NE, 2), ALU.mult))
            link(V.tensor_copy(RG[:, :, 0:NE, 2], r1))
            link(V.tensor_tensor(r2, r1, RG[:, :, 0:NE, 2], ALU.subtract))
            link(V.tensor_copy(RG[:, :, 0:NE, 3], r2))
            link(V.tensor_tensor(r1, r2, RG[:, :, 0:NE, 3], ALU.subtract))
            link(V.tensor_copy(RG[:, :, 0:NE, 4], r1))
            link(V.tensor_tensor(RG[:, :, 0:NE, 0], Mm, bc(tokt, NE, 2), ALU.mult))
            link(V.tensor_tensor(RG[:, :, 0:NE, 1], Mm, bc(tokp, NE, 2), ALU.mult))

            dve.wait_ge(S["u2_rows"], 16 * TT)
            for m in range(2):
                b = done(dve, ("sh", 2 + m))
                taken(dve, ("sh", m))
                takes(V.tensor_tensor(XT[:, 3072 + 512 * m:3584 + 512 * m], b[:], XT[:, 2048 + 512 * m:2560 + 512 * m], ALU.mult),
                      ("sh", 2 + m))
            b = done(dve, ("pos", 0))
            out(V.scalar_tensor_tensor(posm[:, :, 0:NE], a3(b[:, 0:TT * NE], TT), 1.0, Mm, ALU.add, ALU.mult), ("pos", 0))
            link(V.tensor_scalar(posm[:, :, 0:NE], posm[:, :, 0:NE], -1.0, None, ALU.add))
            def make_hot(par, e, first, s):
                V.tensor_tensor(hot[par], bc(first, TT, 1), posm[:, :, bass.ds(e, 1)].broadcast_to((P, TT, P)), ALU.is_equal)\
                    .then_inc(s, 1)

            def take_list(col, s, count, L=ps[5]):
                r = part_row[col % 2]
                V.reduce_sum(gat[:, col:col + 1], L[:, 2:RC], axis=AX.X)
                V.tensor_scalar(r, L[:, 1:2], 8.0 * P, None, ALU.add).then_inc(s[0], 1)
                dve.wait_ge(s[0], count)
                V.scalar_tensor_tensor(idx[:, col:col + 1], L[:, 0:1], float(P), r, ALU.mult, ALU.add).then_inc(s[1], 1)

            def copy_x(par, tr, count, s):
                dve.wait_ge(tr, count)
                V.tensor_copy(xgT[par][:, 4:8], a3(ps[2][:, :], 4)).then_inc(s, 1)

            def hidden(si, count, s):
                dve.wait_ge(si, count)
                V.tensor_tensor(hs, hg, ps[0][:, ED:2 * ED], ALU.mult).then_inc(s, 1)

            def hidden_t(ht, count, s):
                dve.wait_ge(ht, count)
                V.tensor_copy(hTe, a3(ps[3][:, 0:2 * P], 2)).then_inc(s, 1)

            first = iota[:, 0:P]
            em_s = (S["part_rows"], S["list_out"])
            for e in range(2):
                make_hot(e, e, first, S["slot_hot"])
            for e in range(2):
                dve.wait_ge(S["list_done"], e + 1)
                take_list(e, em_s, e + 1, ps[6])
            b = done(dve, ("cnt", 0))
            out(V.tensor_copy(cnt, b[:, 0:NE]), ("cnt", 0))
            link(V.tensor_tensor(ovf.rearrange("p (e b) -> p e b", b=XB), bc(cnt, XB, 2), ovt.rearrange("p (e b) -> p e b", b=XB), ALU.is_gt))
            link(V.memset(ovo, 1.0))
            link(V.tensor_tensor_scan(ovr, ovo, ovf, 0.0, ALU.mult, ALU.add))
            link(V.tensor_copy(ovl[:, 0:1], ovr[:, XB * NE - 1:XB * NE]))
            link(V.scalar_tensor_tensor(ovr, ovr, pp1, ovf, ALU.is_equal, ALU.mult))
            link(V.tensor_tensor(ovf, ovr, ovc, ALU.mult))
            link(V.tensor_reduce(ovl[:, 1:2], ovf, axis=AX.X, op=ALU.add))
            link(V.tensor_tensor(ovf, ovr, ovt, ALU.mult))
            link(V.tensor_reduce(ovl[:, 2:3], ovf, axis=AX.X, op=ALU.add))
            V.tensor_copy(ovi[:], ovl[:, 0:3]).then_inc(S["ov_list"], 1)

            for t in range(TT):
                for n in range(2):
                    b = done(dve, ("dn", t, n))
                    hh = H[:, t, 512 * n:512 * (n + 1)]
                    out(V.tensor_tensor(tmp2, b[:], ADA[:, 5 * DM + 512 * n:5 * DM + 512 * (n + 1)], ALU.mult), ("dn", t, n))
                    link(V.tensor_tensor(hh, hh, tmp2, ALU.add))

            copy_x(0, S["x_tr"], 1, S["x_out_v"])
            pv = posm.rearrange("p t (b r) -> p t b r", r=RING)

            def result(blk, r):
                e = blk * RING + r
                dve.wait_ge(S["expert_done"], e + 1)
                added(dve, blk, r - 2)
                V.tensor_copy(adx[:, r % 2:r % 2 + 1], idx[:, r % RING:r % RING + 1])
                V.tensor_scalar(ye[r % 2][:, 0:512], ps[6][:, :], gat[:, r % RING:r % RING + 1], None, ALU.mult)\
                    .then_inc(S["y_out_v"], 1)

            def step(blk, r):
                e = blk * RING + r
                if follows(blk, r, 2):
                    bl, rr = (blk, r + 2) if r < 2 else (blk + 1, r - 2)
                    V.tensor_tensor(hot[r % 2], bc(first, TT, 1),
                                    pv[:, :, bass.ds(bl, 1), rr].broadcast_to((P, TT, P)), ALU.is_equal).then_inc(S["slot_hot"], 1)
                hidden(S["g_silu"], e + 1, S["h_ok"])
                if follows(blk, r, 1):
                    copy_x((r + 1) % 2, S["x_tr"], e + 2, S["x_out_v"])
                if follows(blk, r, 2):
                    dve.wait_ge(S["list_done"], e + 3)
                    take_list((r + 2) % RING, em_s, e + 3)
                if not is_first(blk, r):
                    result(blk, r - 1)
                hidden_t(S["hT_done"], e + 1, S["hT_out"])

            over_blocks(step, dve)

            def more_hot(j, u):
                e = dve.value_load(ovrow[0:1, bass.ds(j + (MAXOV + 1), 1)], min_val=0, max_val=NE - 1)
                slot0 = dve.value_load(ovrow[0:1, bass.ds(j + 2 * (MAXOV + 1), 1)], min_val=0, max_val=XB * P)
                make_hot(u, e, iota[:, bass.ds(slot0, P)], S["ov_hot"])

            dve.wait_ge(S["ov_row"], 16)
            n_ov = dve.value_load(ovrow[0:1, 0:1], min_val=0, max_val=MAXOV)
            more_hot(0, 0)
            dve.wait_ge(S["ov_ldone"], 1)
            take_list(0, (S["ov_em"], S["ov_idx"]), 1)
            result(NE // RING - 1, RING - 1)
            copy_x(0, S["ov_xt"], 1, S["ov_xv"])
            with dve.Fori(0, 4) as ja:
                with dve.If(n_ov > ja * OVG):
                    with dve.Fori(0, OVG // 2) as jb:
                        jj = ja * (OVG // 2) + jb
                        for u in range(2):
                            j = jj * 2 + u
                            with dve.If(n_ov > j):
                                more_hot(j + 1, 1 - u)
                                dve.wait_ge(S["ov_ldone"], j + 2)
                                dve.wait_ge(S["ov_yo"], j * 2 + 2)
                                take_list(1 - u, (S["ov_em"], S["ov_idx"]), j + 2)
                                hidden(S["ov_silu"], j + 1, S["ov_h"])
                                copy_x(1 - u, S["ov_xt"], j + 2, S["ov_xv"])
                                hidden_t(S["ov_ht"], j + 1, S["ov_hts"])
                                dve.wait_ge(S["ov_y"], j + 3)
                                dve.wait_ge(S["ov_go"], j + 1)
                                V.tensor_copy(adx[:, u:u + 1], idx[:, u:u + 1])
                                V.tensor_scalar(ye[u][:, 0:512], ps[6][:, :], gat[:, u:u + 1], None, ALU.mult).then_inc(S["ov_yo"], 1)

            dve.wait_ge(S["norm_in"], 32)
            for t in range(TT + 1):
                if t < TT:
                    dve.wait_ge(S["sums_joined"], t + 1)
                    x = ut4[:, t]
                    link(V.tensor_tensor(x, x, ADA[:, 5 * DM:6 * DM], ALU.mult))
                    signal(V.tensor_tensor(H[:, t], H[:, t], x, ALU.add), "fin_add", t + 1)
                if t:
                    c = slice(t - 1, t)
                    dve.wait_ge(S["fin_sq"], t)
                    rms_scale(c, 5 + t)
                    V.scalar_tensor_tensor(H[:, t - 1], H[:, t - 1], rstd[:, c], GB[:], ALU.mult, ALU.mult).then_inc(S["final"], 1)

        @block.tensor
        def _(pe):
            mm = nc.tensor.matmul

            def tr(o, i):
                k = i.shape[0]
                return nc.tensor.transpose(o, i, ident[0:k, 0:k])

            def begin(g):
                n = ORDER[g]
                assert n == begun[0], (g, n, begun[0])
                begun[0] += 1
                if n >= NB:
                    taken(pe, AT[n - NB])
                return bank(g)

            def end(ins):
                ins.then_inc(S["group_done"], 1)

            begun = [0]

            def product(g, chunks, rows_=P, cols=512):
                b = begin(g)
                for k, (l, r) in enumerate(chunks):
                    ins = mm(b[0:rows_, 0:cols], l, r, start=(k == 0), stop=(k == len(chunks) - 1))
                return ins

            pe.wait_ge(S["consts"], 1)
            pe.wait_ge(S["lam_in"], 64)
            b = begin(("lam", 0))
            tr(b[:, 0:32], lamn[:, 0:P])
            end(tr(b[:, 32:64], lamn[:, P:2 * P]))
            def ada(n):
                pe.wait_ge(S["ada_sum"], 4 * (n // 4 + 1))
                end(product(("ada", n), [(ones[:], ADA[:, 512 * n:512 * (n + 1)])]))

            def transposed_rows(name, t, src):
                for n in range(2):
                    b = begin((name, t, n))
                    for k in range(4):
                        ins = tr(b[:, P * k:P * (k + 1)], src[:, t, P * (4 * n + k):P * (4 * n + k + 1)])
                    end(ins)

            def projection_t(name, n, w, c0):
                ins = product((name, n), [(w[:, k, c0:c0 + P], uT[:, k]) for k in range(KD)])
                end(ins)

            def s5_build(q):
                pe.wait_ge(S["ba_ok"], q + 1)
                for n in range(2):
                    b = begin(("bT", q, n))
                    for g in range(4):
                        ins = tr(b[:, P * g:P * (g + 1)], BA[:, P * (4 * n + g):P * (4 * n + g + 1)])
                    end(ins)
                pe.wait_ge(S["ca_ok"], q + 1)
                for n in range(2):
                    b = begin(("K", q, n))
                    for g in range(4):
                        gg = 4 * n + g
                        CA = CAb[q % 2]
                        ins = mm(b[0:GH, P * g:P * (g + 1)], Xb[:, GH * (QG * q + gg):GH * (QG * q + gg + 1)],
                                 CA[:, 144 * gg:144 * gg + P], start=True, stop=True)
                    end(ins)

            def s5_apply(q):
                pe.wait_ge(S["u_perm"], q + 1)
                b = begin(("uc", q))
                for g in range(QG):
                    ins = tr(b[:, NC * g:NC * (g + 1)], uperm[:, P * g:P * (g + 1)])
                end(ins)
                taken(pe, ("bT", q, 1))
                taken(pe, ("uc", q))
                b = begin(("v1", q))
                for g in range(QG):
                    ins = mm(b[:, NC * g:NC * (g + 1)], W1[:, P * g:P * (g + 1)], uc[:, NC * g:NC * (g + 1)], start=True, stop=True)
                end(ins)
                b = begin(("v2", q))
                for g in range(QG):
                    for half in range(2):
                        o = 64 * half
                        ins = mm(b[o:o + 64, NC * g:NC * (g + 1)], W1[:, P * g + 64 - o:P * g + P - o], uc[:, NC * g:NC * (g + 1)],
                                 start=True, stop=True)
                end(ins)
                projection_t("gs", q, a3(arrived(pe, ("gs", 0)), 8), P * q)
                pe.wait_ge(S["rotated"], q + 1)
                pe.wait_ge(S["w2_ok"], q + 1)
                pe.wait_ge(S["toeplitz"], 16 * CH * (q + 1))
                CA = CAb[q % 2]
                for n in range(2):
                    b = begin(("y", q, n))
                    for g in range(4):
                        gg = 4 * n + g
                        c, o = slice(NC * gg, NC * (gg + 1)), b[0:NC, P * g:P * (g + 1)]
                        mm(o, GC[:, c], CA[:, 144 * gg + GH:144 * (gg + 1)], start=True, stop=False)
                        mm(o, GS[:, c], W2[:, P * gg:P * (gg + 1)], start=False, stop=False)
                        ins = mm(o, uc[:, c], W3[:, P * gg:P * (gg + 1)], start=False, stop=True)
                    end(ins)

            def indexer(i):
                for h in range(NH):
                    o = 64 * (h % 2)
                    end(product(("idx", i, h), [(qiT[o:o + 64, h // 2, P * i:P * (i + 1)], kiT[o:o + 64, 0:P * (i + 1)])],
                                cols=P * (i + 1)))

            for t in range(TT):
                pe.wait_ge(S["u_tile"], t + 1)
                transposed_rows("uT", t, ut4)
            pe.wait_ge(S["ada_sum"], 4)
            b = begin(("mod", 0))
            for c in range(2 * KD):
                ins = mm(b[:, c:c + 1], ADA[:, P * c:P * (c + 1)], ones[:, 0:1], start=True, stop=True)
            end(ins)
            pe.wait_ge(S["u_ok_v"], KD // 2)
            pe.wait_ge(S["u_ok_s"], KD // 2)
            w = a3(arrived(pe, ("ssm", 0)), 8)
            for t in range(TT):
                end(product(("ssm", t), [(uT[:, k, P * t:P * (t + 1)], w[:, k]) for k in range(KD)]))
            pe.wait_ge(S["ct_in"], 256)
            for j in range(4):
                b = begin(("cT", j))
                tr(b[:, 0:P], cn[:, 2 * j])
                end(tr(b[:, P:2 * P], cn[:, 2 * j + 1]))
            w = a3(arrived(pe, ("misc", 0))[:, 0:8 * 200], 8)
            projection_t("kkT", 0, w, 0)
            end(product(("vwT", 0), [(w[:, k, P:P + 72], uT[:, k]) for k in range(KD)], rows_=72))
            taken(pe, ("vwT", 0))
            b = begin(("vw", 0))
            for t in range(TT):
                ins = tr(b[:, 72 * t:72 * (t + 1)], vwT[:, P * t:P * (t + 1)])
            end(ins)
            w = a3(arrived(pe, ("qi", 0)), 8)
            for m in range(4):
                projection_t("qiT", m, w, P * m)
            taken(pe, ("qiT", 3))

            def gates(name, half):
                w = a3(arrived(pe, (name, half)), 8)
                for d in range(4):
                    projection_t(name, 4 * half + d, w, P * d)

            indexer(1)
            s5_build(0)
            indexer(2)
            s5_apply(0)
            s5_build(1)
            indexer(3)
            s5_apply(1)
            s5_build(2)
            s5_apply(2)
            s5_build(3)
            s5_apply(3)
            w = a3(arrived(pe, ("q", 0)), 8)
            for m in range(4):
                projection_t("qT", m, w, P * m)
            taken(pe, ("y", NQ - 1, 1))
            yv = UB[0:NC, :].rearrange("c (t n) -> c t n", t=CH)
            for m in range(4):
                b = begin(("yT", m))
                for t in range(CH):
                    ins = tr(b[:, NC * t:NC * (t + 1)], yv[:, t, P * m:P * (m + 1)])
                end(ins)
            taken(pe, ("qT", 3))

            def turn_y(i):
                pe.wait_ge(S["y_att"], i + 1)
                b = begin(("yaT", i))
                for m in range(4):
                    ins = tr(b[:, P * m:P * (m + 1)], yat[:, P * m:P * (m + 1)])
                end(ins)

            for i in range(TT):
                w_ = P * (i + 1)

                def logits(h):
                    o = 64 * (h % 2)
                    end(product(("lg", i, h), [(qT[o:o + 64, h // 2, P * i:P * (i + 1)], kT[o:o + 64, 0:w_])], cols=w_))

                def values(h):
                    taken(pe, ("pT", i, h))
                    n = NH * i + h
                    for s in range(i + 1):
                        ins = mm(ps[6 + i % 2][:, HD * h:HD * (h + 1)], pTb[n % 2][:, P * s:P * (s + 1)], vw[:, s, 0:HD],
                                 start=(s == 0), stop=(s == i))
                    ins.then_inc(S["av_done"], 1)

                logits(0)
                logits(1)
                if i >= 2:
                    pe.wait_ge(S["y_att"], i - 1)
                for h in range(NH):
                    if h + 2 < NH:
                        logits(h + 2)
                    n = NH * i + h
                    pe.wait_ge(S["prob"], n + 1)
                    b = begin(("pT", i, h))
                    for s in range(i + 1):
                        ins = tr(b[:, P * s:P * (s + 1)], tb[n % 3][:, P * s:P * (s + 1)])
                    end(ins)
                    if (i, h) in FILL:
                        name, d = FILL[i, h]
                        projection_t(name, d, a3(arrived(pe, (name, d // 4)), 8), P * (d % 4))
                    if i and h == 1:
                        turn_y(i - 1)
                    if h:
                        values(h - 1)
                values(NH - 1)

            taken(pe, ("yT", 3))
            w = a3(arrived(pe, ("glu", 0))[:, 0:2048], 4)
            for m in range(4):
                end(product(("glu", m), [(w[:, k, P * m:P * (m + 1)], yT[:, k]) for k in range(4)]))
            turn_y(TT - 1)

            def branches(half):
                wp = arrived(pe, ("pp", half))
                for d in range(4 * half, 4 * half + 4):
                    for name, y, o in (("ps", y2T, 0), ("pa", yaT, 2048)):
                        w = a3(wp[:, o:o + 2048], 4)
                        end(product((name, d), [(w[:, k, P * (d % 4):P * (d % 4 + 1)], y[:, k]) for k in range(4)]))

            for n in range(4, 12):
                ada(n)
            pe.wait_ge(S["y2_ok"], 4)
            taken(pe, ("yaT", 3))
            branches(0)
            gates("ga", 1)
            branches(1)
            pe.wait_ge(S["mixed"], KD)
            w = [a3(arrived(pe, ("out", n)), 8) for n in range(2)]
            for t in range(TT + 2):
                if t < TT:
                    for n in range(2):
                        end(product(("out", t, n), [(mixT[:, k, P * t:P * (t + 1)], w[n][:, k]) for k in range(KD)]))
                if t >= 2:
                    pe.wait_ge(S["u2_tile"], t - 1)
                    transposed_rows("u2T", t - 2, u2t4)
            taken(pe, ("u2T", TT - 1, 1))
            wd = arrived(pe, ("shd", 0))
            wr = a3(wd[:, 2048:2560], 8)
            end(product(("rt", 0), [(wr[:, k], uT[:, k]) for k in range(KD)], rows_=NE))
            taken(pe, ("rt", 0))
            b = begin(("rtT", 0))
            for t in range(TT):
                ins = tr(b[:, NE * t:NE * (t + 1)], scT64[:, P * t:P * (t + 1)])
            end(ins)
            w = a3(arrived(pe, ("sh", 0)), 8)
            for m in range(4):
                projection_t("sh", m, w, P * m)
            pe.wait_ge(S["slots"], 1)
            b = begin(("pos", 0))
            for t in range(TT):
                for s in range(t + 1):
                    ins = mm(b[:, NE * t:NE * (t + 1)], (ones if s < t else lower)[:], Mm[:, s], start=(s == 0), stop=(s == t))
            end(ins)
            end(product(("cnt", 0), [(ones[:], Mm[:, s]) for s in range(TT)], cols=NE))

            def make_list(par, rhs, s, L=ps[5]):
                for t in range(TT):
                    ins = mm(L[:, 0:RC], hot[par][:, t], rhs(t), start=(t == 0), stop=(t == TT - 1))
                ins.then_inc(s, 1)

            def turn_x(par, s):
                for k in range(KD):
                    ins = tr(ps[1 + k // 4][:, P * (k % 4):P * (k % 4 + 1)], xg[par].rearrange("s (p k) -> s k p", k=KD)[:, k])
                ins.then_inc(s, 1)

            def gate_up(par, r, s):
                for k in range(KD):
                    ins = mm(a3(ps[0][:, :], 2), xgT[par][:, k], wgu[r][:, k], start=(k == 0), stop=(k == KD - 1))
                ins.then_inc(s, 1)

            def turn_h(s):
                for k in range(2):
                    ins = tr(ps[3][:, P * k:P * (k + 1)], hs.rearrange("s (p k) -> s k p", k=2)[:, k])
                ins.then_inc(s, 1)

            def down(r, s):
                for n in range(2):
                    for k in range(2):
                        ins = mm(ps[6 + n][:, :], hTe[:, k], a3(wdn[r], 2)[:, k, 512 * n:512 * (n + 1)], start=(k == 0), stop=(k == 1))
                ins.then_inc(s, 1)

            for e in range(2):
                pe.wait_ge(S["slot_hot"], e + 1)
                if e:
                    pe.wait_ge(S["list_out"], e)
                make_list(e, lambda t: RG[:, t, e, :], S["list_done"], ps[6])
            taken(pe, ("sh", 3))
            wv = a3(wd[:, 0:2048], 2)
            for t in range(TT):
                for n in range(2):
                    end(product(("dn", t, n), [(XT[:, 3072 + 512 * k + P * t:3072 + 512 * k + P * (t + 1)], wv[:, k, 512 * n:512 * (n + 1)]) for k in range(2)]))
            assert begun[0] == len(ORDER)
            taken(pe, ("dn", TT - 1, 1))
            pe.wait_ge(gathered[0], 16)
            turn_x(0, S["x_tr"])
            rgv = RGs.rearrange("p (t b r c) -> p t b r c", t=TT, r=RING, c=RC)

            def down_expert(blk, r):
                e = blk * RING + r
                pe.wait_ge(S["hT_out"], e + 1)
                if r > 0 or not isinstance(blk, int) or blk > 0:
                    pe.wait_ge(S["y_out_s"], e)
                    pe.wait_ge(S["y_out_v"], e)
                down(r % RING, S["expert_done"])

            def step(blk, r):
                e = blk * RING + r
                pe.wait_ge(w_in_sem[r], blk * 48 + 48)
                pe.wait_ge(S["x_out_s"], e + 1)
                pe.wait_ge(S["x_out_v"], e + 1)
                gate_up(r % 2, r, S["gu_done"])
                if follows(blk, r, 1):
                    pe.wait_ge(gathered[(r + 1) % 2], blk * 32 + 16 * ((r + 1) // 2 + 1))
                    turn_x((r + 1) % 2, S["x_tr"])
                if follows(blk, r, 2):
                    pe.wait_ge(S["slot_hot"], e + 3)
                    pe.wait_ge(S["list_out"], e + 2)
                    bl, rr = (blk, r + 2) if r < 2 else (blk + 1, r - 2)
                    make_list(r % 2, lambda t: rgv[:, t, bass.ds(bl, 1), rr, :].rearrange("p b c -> p (b c)"), S["list_done"])
                if not is_first(blk, r):
                    down_expert(blk, r - 1)
                pe.wait_ge(S["h_ok"], e + 1)
                turn_h(S["hT_done"])

            over_blocks(step, pe)

            def more_list(j, u):
                e = pe.value_load(ovrow[0:1, bass.ds(j + (MAXOV + 1), 1)], min_val=0, max_val=NE - 1)
                pe.wait_ge(S["ov_hot"], j + 1)
                make_list(u, lambda t: RG[:, t, bass.ds(e, 1), :].rearrange("p e c -> p (e c)"), S["ov_ldone"])

            pe.wait_ge(S["ov_row"], 16)
            n_ov = pe.value_load(ovrow[0:1, 0:1], min_val=0, max_val=MAXOV)
            more_list(0, 0)
            down_expert(NE // RING - 1, RING - 1)
            pe.wait_ge(S["ov_x"], 16)
            turn_x(0, S["ov_xt"])
            with pe.Fori(0, 4) as ja:
                with pe.If(n_ov > ja * OVG):
                    with pe.Fori(0, OVG // 2) as jb:
                        jj = ja * (OVG // 2) + jb
                        for u in range(2):
                            j = jj * 2 + u
                            with pe.If(n_ov > j):
                                more_list(j + 1, 1 - u)
                                pe.wait_ge(S["ov_xs"], j + 1)
                                pe.wait_ge(S["ov_xv"], j + 1)
                                pe.wait_ge(ov_w[u], jj * 48 + 48)
                                gate_up(u, u, S["ov_gu"])
                                pe.wait_ge(S["ov_x"], j * 16 + 32)
                                turn_x(1 - u, S["ov_xt"])
                                pe.wait_ge(S["ov_h"], j + 1)
                                turn_h(S["ov_ht"])
                                pe.wait_ge(S["ov_hts"], j + 1)
                                pe.wait_ge(S["ov_yo"], j * 2 + 2)
                                down(u, S["ov_y"])


INPUTS = ["x", "c", "w_ada", "b_ada", "norm1_g", "w_in", "ssm_lambda_re", "ssm_lambda_im", "ssm_log_dt", "ssm_b_re",
          "ssm_b_im", "ssm_c_re", "ssm_c_im", "ssm_d", "ssm_w_glu", "ssm_b_glu", "w_proj_ssm", "w_proj_attn", "w_out",
          "norm2_g", "w_router", "router_bias", "w_exp_gate", "w_exp_up", "w_exp_down", "w_sh_gate", "w_sh_up",
          "w_sh_down", "norm_f_g"]


def kernel(**inputs):
    import numpy as np
    import concourse.bacc as bacc
    from concourse.bass_utils import run_bass_kernel_spmd

    nc = bacc.Bacc("TRN2", target_bir_lowering=False, num_devices=1)
    arrays, aps = {}, {}
    for name in INPUTS:
        v = np.ascontiguousarray(inputs[name])
        arrays[f"in_{name}"] = v
        aps[name] = nc.dram_tensor(f"in_{name}", v.shape, mybir.dt.from_np(v.dtype), kind="ExternalInput").ap()
    out = nc.dram_tensor("out_dram", (1, SEQ, DM), F32, kind="ExternalOutput").ap()
    build(nc, aps, out)
    r = run_bass_kernel_spmd(nc, [arrays], core_ids=[0])
    return r.results[0]["out_dram"]
```
